# Optimizing a Trainium2 kernel written in Bass

```python
import math
import jax
import jax.numpy as jnp
from jax import lax
import numpy as np

D_MODEL = 1024
BATCH = 1
SEQ = 1024
DEPTH = 1
DEC_BATCH = 8
DEC_SEQ = 4
PAST_LEN = 4096
PAGE_SIZE = 128

A_HEADS = 8
A_KV_HEADS = 2
A_HEAD_DIM = 64
IDX_HEADS = 4
IDX_DIM = 64
TOPK_MAX = 256
B_HEADS = 4
B_HEAD_DIM = 64
MEM_TOKENS = 256
MEM_HEADS = 4
MEM_HEAD_DIM = 128
D_FF = 2816
CONV_W = 3
NUM_BUCKETS = 32
MAX_DISTANCE = 128
Q_BLOCK = 128
EPS = 1e-6

A_Q = A_HEADS * A_HEAD_DIM
A_KV = A_KV_HEADS * A_HEAD_DIM
IDX_Q = IDX_HEADS * IDX_DIM
B_QK = B_HEADS * 2 * B_HEAD_DIM
B_V = B_HEADS * 2 * B_HEAD_DIM
GROUP_WIDTHS = (A_Q, A_KV, A_KV, IDX_Q, IDX_DIM, IDX_HEADS, B_QK, B_QK, B_V)
D_IN = sum(GROUP_WIDTHS)
MIX_WIDTH = A_Q + B_V
N_BIAS_HEADS = A_HEADS + B_HEADS
MEM_W = MEM_HEADS * MEM_HEAD_DIM

kernel_name = 'hybrid_dsa_diffattn_decoder_step'

def rmsnorm(x, g):
    xf = x.astype(jnp.float32)
    y = xf * lax.rsqrt(jnp.mean(xf * xf, axis=-1, keepdims=True) + EPS)
    return (y * g.astype(jnp.float32)).astype(x.dtype)

def rel_bucket(dist):
    n = jnp.maximum(dist, 0)
    max_exact = NUM_BUCKETS // 2
    nf = jnp.maximum(n, 1).astype(jnp.float32)
    log_b = jnp.log(nf / max_exact) / math.log(MAX_DISTANCE / max_exact) * (NUM_BUCKETS - max_exact)
    large = jnp.minimum(max_exact + log_b.astype(jnp.int32), NUM_BUCKETS - 1)
    return jnp.where(n < max_exact, n, large)

def project_groups(xn, w_in, a_qn, a_kn, b_qn, b_kn):
    b, t, _ = xn.shape
    proj = xn @ w_in
    cuts, acc = [], 0
    for w in GROUP_WIDTHS[:-1]:
        acc += w
        cuts.append(acc)
    qa, ka, va, qi, ki, wi, qb, kb, vb = jnp.split(proj, cuts, axis=-1)
    qa = rmsnorm(qa.reshape(b, t, A_HEADS, A_HEAD_DIM), a_qn)
    ka = rmsnorm(ka.reshape(b, t, A_KV_HEADS, A_HEAD_DIM), a_kn)
    va = va.reshape(b, t, A_KV_HEADS, A_HEAD_DIM)
    qi = qi.reshape(b, t, IDX_HEADS, IDX_DIM)
    qb = rmsnorm(qb.reshape(b, t, B_HEADS, 2, B_HEAD_DIM), b_qn)
    kb = rmsnorm(kb.reshape(b, t, B_HEADS, 2, B_HEAD_DIM), b_kn)
    vb = vb.reshape(b, t, B_HEADS, 2 * B_HEAD_DIM)
    return qa, ka, va, qi, ki, wi, qb, kb, vb

def indexer_scores(qi, wi, ki):
    dots = jnp.einsum('bqhd,bkd->bqhk', qi, ki).astype(jnp.float32) * (IDX_DIM ** -0.5)
    return jnp.einsum('bqhk,bqh->bqk', jax.nn.relu(dots), wi.astype(jnp.float32) * (IDX_HEADS ** -0.5))

def select_keys(scores, qpos, n_keys, topk):
    kpos = jnp.arange(n_keys)
    causal = kpos[None, None, :] <= qpos[None, :, None]
    _, idx = lax.top_k(jnp.where(causal, scores, -jnp.inf), topk)
    valid = idx <= qpos[None, :, None]
    return idx, valid

def dsa_core(q, k_sel, v_sel, valid, dist, bias_a):
    b, nq, kk = valid.shape
    rep = A_HEADS // A_KV_HEADS
    qg = q.reshape(b, nq, A_KV_HEADS, rep, A_HEAD_DIM)
    logits = jnp.einsum('bqgrd,bqkgd->bqgrk', qg, k_sel).astype(jnp.float32) * (A_HEAD_DIM ** -0.5)
    bias = bias_a[rel_bucket(dist)].astype(jnp.float32)
    bias = bias.reshape(b, nq, kk, A_KV_HEADS, rep).transpose(0, 1, 3, 4, 2)
    logits = jnp.where(valid[:, :, None, None, :], logits + bias, -jnp.inf)
    p = jax.nn.softmax(logits, axis=-1).astype(v_sel.dtype)
    o = jnp.einsum('bqgrk,bqkgd->bqgrd', p, v_sel)
    return o.reshape(b, nq, A_Q)

def dsa_prompt(qa, ka, va, qi, ki, wi, bias_a):
    b, s = qa.shape[:2]
    topk = min(TOPK_MAX, s // 4)
    b_ix = jnp.arange(b)[:, None, None]

    def block(i):
        q0 = i * Q_BLOCK
        qpos = q0 + jnp.arange(Q_BLOCK)
        sl = lambda a: lax.dynamic_slice_in_dim(a, q0, Q_BLOCK, axis=1)
        idx, valid = select_keys(indexer_scores(sl(qi), sl(wi), ki), qpos, s, topk)
        return dsa_core(sl(qa), ka[b_ix, idx], va[b_ix, idx], valid, qpos[None, :, None] - idx, bias_a)

    out = lax.map(block, jnp.arange(s // Q_BLOCK))
    return out.transpose(1, 0, 2, 3).reshape(b, s, A_Q)

def gather_pages(pool, page_table):
    rows = pool[page_table]
    return rows.reshape((page_table.shape[0], -1) + pool.shape[2:])

def gather_selected(pool, page_table, new_rows, idx, past):
    page = pool.shape[1]
    b_ix = jnp.arange(idx.shape[0])[:, None, None]
    ip = jnp.minimum(idx, past - 1)
    from_pool = pool[page_table[b_ix, ip // page], ip % page].astype(new_rows.dtype)
    from_new = new_rows[b_ix, jnp.clip(idx - past, 0, new_rows.shape[1] - 1)]
    in_past = (idx < past).reshape(idx.shape + (1,) * (from_pool.ndim - idx.ndim))
    return jnp.where(in_past, from_pool, from_new)

def dsa_sample(qa, ka, va, qi, ki, wi, cache_k, cache_v, cache_ik, page_table, bias_a):
    t = qa.shape[1]
    past = page_table.shape[1] * cache_k.shape[1]
    n_keys = past + t
    qpos = past + jnp.arange(t)
    ki_all = jnp.concatenate([gather_pages(cache_ik, page_table).astype(ki.dtype), ki], axis=1)
    idx, valid = select_keys(indexer_scores(qi, wi, ki_all), qpos, n_keys, min(TOPK_MAX, n_keys // 4))
    k_sel = gather_selected(cache_k, page_table, ka, idx, past)
    v_sel = gather_selected(cache_v, page_table, va, idx, past)
    return dsa_core(qa, k_sel, v_sel, valid, qpos[None, :, None] - idx, bias_a)

def diff_lambda_value(lam_p, lam_init):
    lp = lam_p.astype(jnp.float32)
    return jnp.exp(jnp.sum(lp[0] * lp[1])) - jnp.exp(jnp.sum(lp[2] * lp[3])) + lam_init

def diff_core(q, k, v, qpos, kpos, bias_b, lam, lam_init, subln_g):
    b, nq = q.shape[:2]
    logits = jnp.einsum('bqhcd,bkhcd->bhcqk', q, k).astype(jnp.float32) * (B_HEAD_DIM ** -0.5)
    bias = bias_b[rel_bucket(qpos[:, None] - kpos[None, :])].astype(jnp.float32)
    logits = logits + bias.transpose(2, 0, 1)[None, :, None]
    causal = kpos[None, :] <= qpos[:, None]
    p = jax.nn.softmax(jnp.where(causal, logits, -jnp.inf), axis=-1)
    w = (p[:, :, 0] - lam * p[:, :, 1]).astype(v.dtype)
    o = jnp.einsum('bhqk,bkhe->bqhe', w, v)
    o = rmsnorm(o, subln_g) * (1.0 - lam_init)
    return o.reshape(b, nq, B_V)

def diff_prompt(qb, kb, vb, bias_b, lam, lam_init, subln_g):
    b, s = qb.shape[:2]
    kpos = jnp.arange(s)

    def block(i):
        q0 = i * Q_BLOCK
        qblk = lax.dynamic_slice_in_dim(qb, q0, Q_BLOCK, axis=1)
        return diff_core(qblk, kb, vb, q0 + jnp.arange(Q_BLOCK), kpos, bias_b, lam, lam_init, subln_g)

    out = lax.map(block, jnp.arange(s // Q_BLOCK))
    return out.transpose(1, 0, 2, 3).reshape(b, s, B_V)

def diff_sample(qb, kb, vb, cache_k, cache_v, page_table, bias_b, lam, lam_init, subln_g):
    t = qb.shape[1]
    past = page_table.shape[1] * cache_k.shape[1]
    k_all = jnp.concatenate([gather_pages(cache_k, page_table).astype(kb.dtype), kb], axis=1)
    v_all = jnp.concatenate([gather_pages(cache_v, page_table).astype(vb.dtype), vb], axis=1)
    return diff_core(qb, k_all, v_all, past + jnp.arange(t), jnp.arange(past + t), bias_b, lam, lam_init, subln_g)

def memory_kv(mem, g_src, w_kv, k_norm_g):
    b, m, _ = mem.shape
    kv = rmsnorm(mem, g_src) @ w_kv
    k, v = jnp.split(kv, 2, axis=-1)
    k = rmsnorm(k.reshape(b, m, MEM_HEADS, MEM_HEAD_DIM), k_norm_g)
    return k, v.reshape(b, m, MEM_HEADS, MEM_HEAD_DIM)

def memory_attend(xn, w_q, q_norm_g, mk, mv, w_o):
    b, t, _ = xn.shape
    q = rmsnorm((xn @ w_q).reshape(b, t, MEM_HEADS, MEM_HEAD_DIM), q_norm_g)
    logits = jnp.einsum('bqhd,bmhd->bhqm', q, mk.astype(q.dtype)).astype(jnp.float32) * (MEM_HEAD_DIM ** -0.5)
    p = jax.nn.softmax(logits, axis=-1).astype(q.dtype)
    o = jnp.einsum('bhqm,bmhd->bqhd', p, mv.astype(q.dtype))
    return o.reshape(b, t, MEM_W) @ w_o

def conv_ffn(xn, conv_state, w_up, w_gate, conv_w, conv_b, w_down):
    t = xn.shape[1]
    g = xn @ w_gate
    gb = jnp.concatenate([conv_state.astype(g.dtype), g], axis=1)
    gc = conv_b + sum(conv_w[j] * gb[:, j:j + t] for j in range(CONV_W))
    y = (jax.nn.silu(gc) * (xn @ w_up)) @ w_down
    return y, gb[:, t:]

def setup_inputs(seed: int = 0) -> dict:
    key = jax.random.key(seed)
    keys = list(jax.random.split(key, 48))

    def nrm(shape, scale):
        return scale * jax.random.normal(keys.pop(), shape, jnp.float32)

    def gain(shape):
        return 1.0 + 0.01 * jax.random.normal(keys.pop(), shape, jnp.float32)

    n_pages = PAST_LEN // PAGE_SIZE
    n_pool = (DEC_BATCH * n_pages * 5) // 4
    page_table = jax.random.permutation(keys.pop(), n_pool)[: DEC_BATCH * n_pages].reshape(DEC_BATCH, n_pages).astype(jnp.int32)
    pool = (DEPTH, n_pool, PAGE_SIZE)
    return {
        'x_prompt': nrm((BATCH, SEQ, D_MODEL), 1.0),
        'x_sample': nrm((DEC_BATCH, DEC_SEQ, D_MODEL), 1.0),
        'mem_prompt': nrm((BATCH, MEM_TOKENS, D_MODEL), 1.0),
        'cache_a_k': nrm(pool + (A_KV_HEADS, A_HEAD_DIM), 1.0),
        'cache_a_v': nrm(pool + (A_KV_HEADS, A_HEAD_DIM), 1.0),
        'cache_idx_k': nrm(pool + (IDX_DIM,), 1.0),
        'cache_b_k': nrm(pool + (B_HEADS, 2, B_HEAD_DIM), 1.0),
        'cache_b_v': nrm(pool + (B_HEADS, 2 * B_HEAD_DIM), 1.0),
        'cache_mem_k': nrm((DEPTH, DEC_BATCH, MEM_TOKENS, MEM_HEADS, MEM_HEAD_DIM), 1.0),
        'cache_mem_v': nrm((DEPTH, DEC_BATCH, MEM_TOKENS, MEM_HEADS, MEM_HEAD_DIM), 1.0),
        'state_ffn_conv': nrm((DEPTH, DEC_BATCH, CONV_W - 1, D_FF), 1.0),
        'page_table': page_table,
        'rel_bias': nrm((NUM_BUCKETS, N_BIAS_HEADS), 0.5),
        'norm_mix': gain((DEPTH, D_MODEL)),
        'w_in': nrm((DEPTH, D_MODEL, D_IN), D_MODEL ** -0.5),
        'a_q_norm': gain((DEPTH, A_HEAD_DIM)),
        'a_k_norm': gain((DEPTH, A_HEAD_DIM)),
        'b_q_norm': gain((DEPTH, B_HEAD_DIM)),
        'b_k_norm': gain((DEPTH, B_HEAD_DIM)),
        'diff_lambda': nrm((DEPTH, 4, B_HEAD_DIM), 0.1),
        'diff_subln': gain((DEPTH, 2 * B_HEAD_DIM)),
        'w_out': nrm((DEPTH, MIX_WIDTH, D_MODEL), MIX_WIDTH ** -0.5),
        'norm_mem_x': gain((DEPTH, D_MODEL)),
        'norm_mem_src': gain((DEPTH, D_MODEL)),
        'w_mem_q': nrm((DEPTH, D_MODEL, MEM_W), D_MODEL ** -0.5),
        'w_mem_kv': nrm((DEPTH, D_MODEL, 2 * MEM_W), D_MODEL ** -0.5),
        'mem_q_norm': gain((DEPTH, MEM_HEAD_DIM)),
        'mem_k_norm': gain((DEPTH, MEM_HEAD_DIM)),
        'w_mem_o': nrm((DEPTH, MEM_W, D_MODEL), MEM_W ** -0.5),
        'norm_ffn': gain((DEPTH, D_MODEL)),
        'w_up': nrm((DEPTH, D_MODEL, D_FF), D_MODEL ** -0.5),
        'w_gate': nrm((DEPTH, D_MODEL, D_FF), D_MODEL ** -0.5),
        'ffn_conv_w': nrm((DEPTH, CONV_W, D_FF), CONV_W ** -0.5),
        'ffn_conv_b': nrm((DEPTH, D_FF), 0.01),
        'w_down': nrm((DEPTH, D_FF, D_MODEL), D_FF ** -0.5),
    }

def reference(x_prompt, x_sample, mem_prompt, cache_a_k, cache_a_v, cache_idx_k, cache_b_k, cache_b_v,
              cache_mem_k, cache_mem_v, state_ffn_conv, page_table, rel_bias, norm_mix, w_in,
              a_q_norm, a_k_norm, b_q_norm, b_k_norm, diff_lambda, diff_subln, w_out,
              norm_mem_x, norm_mem_src, w_mem_q, w_mem_kv, mem_q_norm, mem_k_norm, w_mem_o,
              norm_ffn, w_up, w_gate, ffn_conv_w, ffn_conv_b, w_down):
    bias_a = rel_bias[:, :A_HEADS]
    bias_b = rel_bias[:, A_HEADS:]
    yp, ys = x_prompt, x_sample
    pak, pav, pik, pbk, pbv, pmk, pmv, pcv = [], [], [], [], [], [], [], []
    sak, sav, sik, sbk, sbv, scv = [], [], [], [], [], []
    for l in range(DEPTH):
        lam_init = 0.8 - 0.6 * math.exp(-0.3 * l)
        lam = diff_lambda_value(diff_lambda[l], lam_init)
        qk_gains = (a_q_norm[l], a_k_norm[l], b_q_norm[l], b_k_norm[l])

        qa, ka, va, qi, ki, wi, qb, kb, vb = project_groups(rmsnorm(yp, norm_mix[l]), w_in[l], *qk_gains)
        mix = jnp.concatenate([dsa_prompt(qa, ka, va, qi, ki, wi, bias_a),
                               diff_prompt(qb, kb, vb, bias_b, lam, lam_init, diff_subln[l])], axis=-1)
        yp = yp + mix @ w_out[l]
        mk, mv = memory_kv(mem_prompt, norm_mem_src[l], w_mem_kv[l], mem_k_norm[l])
        yp = yp + memory_attend(rmsnorm(yp, norm_mem_x[l]), w_mem_q[l], mem_q_norm[l], mk, mv, w_mem_o[l])
        zero_conv = jnp.zeros((yp.shape[0], CONV_W - 1, D_FF), yp.dtype)
        f, conv_p = conv_ffn(rmsnorm(yp, norm_ffn[l]), zero_conv, w_up[l], w_gate[l], ffn_conv_w[l], ffn_conv_b[l], w_down[l])
        yp = yp + f
        pak.append(ka); pav.append(va); pik.append(ki); pbk.append(kb); pbv.append(vb)
        pmk.append(mk); pmv.append(mv); pcv.append(conv_p)

        qa, ka, va, qi, ki, wi, qb, kb, vb = project_groups(rmsnorm(ys, norm_mix[l]), w_in[l], *qk_gains)
        mix = jnp.concatenate([
            dsa_sample(qa, ka, va, qi, ki, wi, cache_a_k[l], cache_a_v[l], cache_idx_k[l], page_table, bias_a),
            diff_sample(qb, kb, vb, cache_b_k[l], cache_b_v[l], page_table, bias_b, lam, lam_init, diff_subln[l])], axis=-1)
        ys = ys + mix @ w_out[l]
        ys = ys + memory_attend(rmsnorm(ys, norm_mem_x[l]), w_mem_q[l], mem_q_norm[l], cache_mem_k[l], cache_mem_v[l], w_mem_o[l])
        f, conv_s = conv_ffn(rmsnorm(ys, norm_ffn[l]), state_ffn_conv[l], w_up[l], w_gate[l], ffn_conv_w[l], ffn_conv_b[l], w_down[l])
        ys = ys + f
        sak.append(ka); sav.append(va); sik.append(ki); sbk.append(kb); sbv.append(vb); scv.append(conv_s)

    return (yp, ys,
            jnp.stack(pak), jnp.stack(pav), jnp.stack(pik), jnp.stack(pbk), jnp.stack(pbv),
            jnp.stack(pmk), jnp.stack(pmv), jnp.stack(pcv),
            jnp.stack(sak), jnp.stack(sav), jnp.stack(sik), jnp.stack(sbk), jnp.stack(sbv), jnp.stack(scv))


_drawn_inputs = setup_inputs


def setup_inputs(seed=0):
    import zlib

    import numpy as np

    out = dict(_drawn_inputs(seed))
    spreads = {}
    factors = {'norm_mix': 4.613,
     'a_q_norm': 8.0,
     'a_k_norm': 7.219,
     'b_q_norm': 8.0,
     'b_k_norm': 5.998,
     'diff_lambda': 4.06,
     'diff_subln': 8.0,
     'norm_mem_x': 8.0,
     'norm_mem_src': 5.648,
     'mem_q_norm': 8.0,
     'mem_k_norm': 5.904,
     'norm_ffn': 5.843,
     'ffn_conv_b': 8.0}
    for name, (base, spread) in spreads.items():
        noise = np.random.default_rng([zlib.crc32(name.encode()), seed]).standard_normal(out[name].shape)
        drawn = base * np.exp(spread * noise) if base else spread * noise
        out[name] = jnp.asarray(drawn.astype(out[name].dtype))
    for name, factor in factors.items():
        out[name] = (out[name] * factor).astype(out[name].dtype)
    return out
```

```python
import math
from contextlib import ExitStack

import numpy as np
import concourse.bass as bass
from concourse import mybir

F32 = mybir.dt.float32
BF16 = mybir.dt.bfloat16
I32 = mybir.dt.int32
ACT = mybir.ActivationFunctionType
ALU = mybir.AluOpType
AX = mybir.AxisListType

P = 128
D = 1024
KC = D // P
SEQ = 1024
NB = SEQ // P
DEC_B, DEC_T = 8, 4
NS = DEC_B * DEC_T
NT = NB + 1
NTOK = SEQ + NS
PAST = 4096
PAGE = 128
TOPK = 256
A_H, A_KV, B_H, HD, IDX_H = 8, 2, 4, 64, 4
MEM, MEM_H, MEM_D = 256, 4, 128
DFF = 2816
FT = DFF // P
NBUCKET = 32
EPS = 1e-6
NEG = -1e30
GONE = -3e38
LAM0 = 0.8 - 0.6 * math.exp(0.0)
CH = 512
NCH = PAST // CH
RK = 4
KEYS_S = PAST + NS


def rows_of(t):
    return NS if t == NB else P


def rel_bucket(n):
    n = np.maximum(n, 0)
    half = NBUCKET // 2
    lg = np.log(np.maximum(n, 1).astype(np.float32) / half) / math.log(128 / half) * (NBUCKET - half)
    return np.where(n < half, n, np.minimum(half + lg.astype(np.int32), NBUCKET - 1))


def far_one_hot(dist):
    hot = (np.arange(NBUCKET)[:, None] == rel_bucket(dist)[None]).astype(np.float32)
    hot[NBUCKET - 1] -= 1.0
    return hot * (dist >= 0)


def shape_constants():
    p = np.arange(P)
    r, j = p % 32, p // 32
    t = p % 4
    q = np.arange(NS)
    qb, qt = q // DEC_T, q % DEC_T
    c = {}
    c["causal"] = np.where(p[None] > p[:, None], NEG, 0.0)
    c["oh_prompt"] = far_one_hot(255 - np.arange(3 * P))
    near = np.arange(P)
    oh = np.zeros((DEC_T, NBUCKET, P + NS), np.float32)
    for tt in range(DEC_T):
        oh[tt, :, :P] = far_one_hot(P + tt - near)
        oh[tt, :, P:] = far_one_hot(tt - qt)
    c["oh_sample"] = oh.reshape(P, P + NS)
    c["t_of_row"] = (p[:, None] // 32 == np.arange(4)[None]).astype(np.float32)
    for g in range(2):
        own = (qb[None] == 4 * g + j[:, None])
        c[f"new_mask{g}"] = np.where(own & (qt[None] <= t[:, None]), 0.0, NEG)
        c[f"row_to_tok{g}"] = (own & (qt[None] == t[:, None])).astype(np.float32)
        c[f"tok_to_row{g}"] = c[f"row_to_tok{g}"].T
    c["idx_mask"] = np.where((qb[None] == qb[:, None]) & (qt[None] <= qt[:, None]), 0.0, NEG)
    c["head_i"] = (r[:, None] // 4 == np.arange(4)[None]).astype(np.float32)
    c["head_a"] = (r[:, None] // 4 == np.arange(8)[None]).astype(np.float32)
    c["head_b"] = (r[:, None] // 8 == np.arange(4)[None]).astype(np.float32)
    c["branch"] = (((r[:, None] // 4) % 2) == np.arange(2)[None]).astype(np.float32)
    c["group"] = (j[:, None] == np.arange(4)[None]).astype(np.float32)
    c["sub_row"] = r[:, None].astype(np.float32)
    return {k: np.asarray(v, np.float32) for k, v in c.items()}


def pack_constants():
    c = shape_constants()
    total = sum(v.shape[1] for v in c.values())
    out = np.zeros((P, total), np.float32)
    at, o = {}, 0
    for k, v in c.items():
        out[: v.shape[0], o : o + v.shape[1]] = v
        at[k] = (v.shape[0], o, v.shape[1])
        o += v.shape[1]
    return out, at


class Memory:
    pass


class Chunk:

    def __init__(self, off, width, norm=None, copies=None, gains=None, sources=None, targets=None,
                 stores=lambda t, n, s: [], arrange=None):
        self.off, self.width, self.norm, self.copies, self.gains = off, width, norm, copies, gains
        self.sources, self.targets, self.stores, self.arrange = sources, targets, stores, arrange


class Chain:

    def __init__(self, eng, sem):
        self.eng, self.sem, self.n = eng, sem, 0

    def __call__(self, ins):
        self.n += 1
        ins.then_inc(self.sem, 1)
        self.eng.wait_ge(self.sem, self.n)


class Stage:

    def __init__(self, nc, ctx, name):
        self.nc, self.ctx, self.name = nc, ctx, name

    def sb(self, n, shape, dt=F32):
        return self.ctx.enter_context(self.nc.sbuf_tensor(f"{self.name}_{n}", shape, dt))

    def sem(self, n):
        s = self.ctx.enter_context(self.nc.semaphore(f"{self.name}_{n}"))
        Stage.ended.append(s)
        return s

    def store_sem(self, n):
        return Stage.stores.get(f"{self.name}_{n}")


def clear_semaphores(nc):
    with nc.Block() as block:
        @block.gpsimd
        def _(pool):
            for s in Stage.ended:
                pool.sem_clear(s)
    Stage.ended.clear()


COL = {}
_n = 0
for _name, _k in (("norm_mix", KC), ("norm_mem_x", KC), ("norm_mem_src", KC), ("norm_ffn", KC),
                  ("a_q", 1), ("b_q", 1), ("mem_q", 1), ("conv_b", FT), ("conv_w", 3 * FT)):
    COL[_name] = _n
    _n += _k
NCOL = _n


def load_x(eng, io, M):
    for t in range(NB):
        eng.dma_start(M.X[:, t, :], io["x_prompt"][0, t * P:(t + 1) * P, :]).then_inc(M.x_loaded[t], 16)
    eng.dma_start(M.X[0:NS, NB, :], io["x_sample"].rearrange("b t d -> (b t) d")).then_inc(M.x_loaded[NB], 16)


def setup_stage(nc, io, M, K):
    with ExitStack() as ctx:
        S = Stage(nc, ctx, "setup")
        rows = S.sb("rows", [NCOL, P])
        rb32 = S.sb("rb32", [NBUCKET, 12])
        rb4 = S.sb("rb4", [P, 12])
        rbw = S.sb("rbw", [NBUCKET, 12, P])
        lrow = S.sb("lrow", [P, 2, P])
        toe = S.sb("toe", [P, 12, 3 * P])
        pt_i = S.sb("pt_i", [P, DEC_B * 32], I32)
        pt_f = S.sb("pt_f", [P, DEC_B * NCH, 4])
        ix_f = S.sb("ix_f", [P, DEC_B * NCH])
        lamv = S.sb("lamv", [P, 4, HD])
        lamw = S.sb("lamw", [P, 2, HD])
        lam2 = S.sb("lam2", [P, 2])
        lam2e = S.sb("lam2e", [P, 2])
        lam = S.sb("lam", [P, 1])
        bias_scr = nc.dram_tensor("bias_scratch", [12, P * 3 * P], F32)
        loaded = S.sem("loaded")
        toe_out, toe_in = S.sem("toe_out"), S.sem("toe_in")
        chain, dve_ready = S.sem("chain"), S.sem("dve_ready")
        cols_tr, bias_mm, bias_cp, samp_mm, lam_exp = (S.sem(n) for n in (
            "cols_tr", "bias_mm", "bias_cp", "samp_mm", "lam_exp"))
        nloads = [0]

        with nc.Block() as block:
            @block.sync
            def _(sp):
                def load(dst, src):
                    sp.dma_start(dst, src).then_inc(loaded, 16)
                    nloads[0] += 1
                load(M.ident[:], io["ident"][:])
                load(M.const[:], io["consts"][:])
                load(rb32[:], io["rel_bias"][:])
                for t in range(4):
                    load(rb4[32 * t:32 * t + 32, :], io["rel_bias"][:])
                def rowload(name, src, k):
                    load(rows[COL[name]:COL[name] + k, :], src.rearrange("(k p) -> k p", p=P))
                rowload("norm_mix", io["norm_mix"][0], KC)
                rowload("norm_mem_x", io["norm_mem_x"][0], KC)
                rowload("norm_mem_src", io["norm_mem_src"][0], KC)
                rowload("norm_ffn", io["norm_ffn"][0], KC)
                for e in range(2):
                    load(rows[COL["a_q"]:COL["a_q"] + 1, 64 * e:64 * e + 64], io["a_q_norm"][:])
                    load(rows[COL["b_q"]:COL["b_q"] + 1, 64 * e:64 * e + 64], io["b_q_norm"][:])
                load(rows[COL["mem_q"]:COL["mem_q"] + 1, :], io["mem_q_norm"][:])
                rowload("conv_b", io["ffn_conv_b"][0], FT)
                load(rows[COL["conv_w"]:COL["conv_w"] + 3 * FT, :],
                     io["ffn_conv_w"][0].rearrange("w (k p) -> (w k) p", p=P))
                load(M.gain_ak[:], io["a_k_norm"][0].partition_broadcast(P))
                load(M.gain_bk[:], io["b_k_norm"][0].partition_broadcast(P))
                load(M.gain_mk[:], io["mem_k_norm"][0].partition_broadcast(P))
                load(M.gain_sub[:], io["diff_subln"][0].partition_broadcast(P))
                load(lamv[:], io["diff_lambda"][0].partition_broadcast(P))
                load(pt_i[:], io["page_table"].rearrange("b n -> (b n)").partition_broadcast(P))
                sp.wait_ge(bias_cp, 12)
                sp.dma_start(bias_scr.ap().rearrange("h (p c) -> p h c", p=P), toe[:]).then_inc(toe_out, 16)
                sp.wait_ge(toe_out, 16)
                shifted = bass.AP(bias_scr, P - 1, [[3 * P - 1, P], [P * 3 * P, 12], [1, 2 * P]])
                sp.dma_start(M.bias_p[:], shifted).then_inc(toe_in, 16)

            total = nloads[0] * 16

            @block.scalar
            def _(act):
                load_x(act, io, M)
                for h in range(12):
                    act.wait_ge(bias_mm, h + 1)
                    nc.scalar.copy(toe[:, h, :], M.PS[:, h % 4, 0:3 * P]).then_inc(bias_cp, 1)
                act.wait_ge(dve_ready, 3)
                nc.scalar.activation(lam2e[:], lam2[:], ACT.Exp).then_inc(lam_exp, 1)

            @block.vector
            def _(dve):
                link = Chain(dve, chain)
                link(nc.vector.memset(M.neg_half[:], -0.5))
                link(nc.vector.memset(M.QBA[:], 0.0))
                link(nc.vector.memset(M.QBB[:], 0.0))
                link(nc.vector.memset(M.QBI[:], 0.0))
                dve.wait_ge(loaded, total)
                link(nc.vector.tensor_copy(M.ident_b[:], K("ident")))
                for g in range(2):
                    link(nc.vector.tensor_copy(M.tok_to_row_b[:, g, :], K(f"tok_to_row{g}")))
                link(nc.vector.tensor_copy(rbw[:], rb32[:].unsqueeze(2).to_broadcast([NBUCKET, 12, P])))
                nc.vector.memset(M.zero_col[:], 0.0).then_inc(dve_ready, 1)
                for j in range(4):
                    link(nc.vector.tensor_tensor(
                        lrow[:, 0, 32 * j:32 * j + 32].rearrange("p (h t) -> p h t", t=4),
                        rb4[:, 0:A_H].unsqueeze(2).to_broadcast([P, A_H, 4]),
                        K("t_of_row").unsqueeze(1).to_broadcast([P, A_H, 4]), ALU.mult))
                    for c in range(2):
                        link(nc.vector.tensor_tensor(
                            lrow[:, 1, 32 * j:32 * j + 32].rearrange("p (h c t) -> p c h t", c=2, t=4)[:, c],
                            rb4[:, A_H:12].unsqueeze(2).to_broadcast([P, B_H, 4]),
                            K("t_of_row").unsqueeze(1).to_broadcast([P, B_H, 4]), ALU.mult))
                nc.vector.memset(M.zero_col[:], 0.0).then_inc(dve_ready, 1)
                for k in range(2):
                    link(nc.vector.tensor_tensor(lamw[:, k, :], lamv[:, 2 * k, :], lamv[:, 2 * k + 1, :], ALU.mult))
                nc.vector.tensor_reduce(lam2[:], lamw[:], axis=AX.X, op=ALU.add).then_inc(dve_ready, 1)
                dve.wait_ge(lam_exp, 1)
                link(nc.vector.tensor_tensor(lam[:], lam2e[:, 0:1], lam2e[:, 1:2], ALU.subtract))
                link(nc.vector.tensor_scalar(M.neg_lam[:], lam[:], LAM0, -1.0, ALU.add, ALU.mult))
                link(nc.vector.tensor_scalar(M.branch_coef[:], K("branch")[:, 1:2], M.neg_lam[:], None, ALU.mult))
                link(nc.vector.tensor_tensor(M.branch_coef[:], M.branch_coef[:], K("branch")[:, 0:1], ALU.add))
                link(nc.vector.tensor_scalar(M.gain_sub[:], M.gain_sub[:], 1.0 - LAM0, None, ALU.mult))
                link(nc.vector.tensor_copy(pt_f[:].rearrange("p a b -> p (a b)"), pt_i[:]))
                link(nc.vector.tensor_scalar(ix_f[:], pt_f[:, :, 0], K("group")[:, 0:1], None, ALU.mult))
                for i in range(1, 4):
                    link(nc.vector.scalar_tensor_tensor(ix_f[:], pt_f[:, :, i], K("group")[:, i:i + 1], ix_f[:],
                                                        ALU.mult, ALU.add))
                link(nc.vector.tensor_scalar(ix_f[:], ix_f[:], float(PAGE // RK), K("sub_row"), ALU.mult, ALU.add))
                link(nc.vector.tensor_copy(M.gather_row[:], ix_f[:]))
                dve.wait_ge(cols_tr, 1)
                link(nc.vector.tensor_copy(M.cols[:], M.PS[:, 4, 0:NCOL]))
                for n in ("a_q", "b_q"):
                    link(nc.vector.tensor_scalar(M.cols[:, COL[n]:COL[n] + 1], M.cols[:, COL[n]:COL[n] + 1],
                                                 HD ** -0.5, None, ALU.mult))
                dve.wait_ge(samp_mm, 1)
                for k in range(2):
                    link(nc.vector.tensor_copy(M.bias_s[:, k, :], M.PS[:, 5 + k, 0:P]))
                    for g in range(2):
                        link(nc.vector.tensor_tensor(M.bias_new[:, k, g, :], M.PS[:, 5 + k, P:P + NS],
                                                     K(f"new_mask{g}"), ALU.add))
                dve.wait_ge(toe_in, 16)
                link(nc.vector.tensor_tensor(M.bias_p[:, :, P:2 * P], M.bias_p[:, :, P:2 * P],
                                             K("causal").unsqueeze(1).to_broadcast([P, 12, P]), ALU.add))

            @block.tensor
            def _(pe):
                pe.wait_ge(loaded, total)
                nc.tensor.transpose(M.PS[:, 4, 0:NCOL], rows[:], K("ident")[0:NCOL, 0:NCOL]).then_inc(cols_tr, 1)
                pe.wait_ge(dve_ready, 1)
                for h in range(12):
                    if h >= 4:
                        pe.wait_ge(bias_cp, h - 3)
                    nc.tensor.matmul(M.PS[:, h % 4, 0:3 * P], rbw[:, h, :], K("oh_prompt"),
                                     start=True, stop=True).then_inc(bias_mm, 1)
                pe.wait_ge(dve_ready, 2)
                for k in range(2):
                    last = nc.tensor.matmul(M.PS[:, 5 + k, 0:P + NS], lrow[:, k, :], K("oh_sample"),
                                            start=True, stop=True)
                last.then_inc(samp_mm, 1)


def norm_transpose_stage(nc, M, K, name, X, tiles, out, col, wait_x=None):
    with ExitStack() as ctx:
        S = Stage(nc, ctx, name)
        junk = S.sb("junk", [P, D], BF16)
        ss = S.sb("ss", [P, NT])
        ms = S.sb("ms", [P, NT])
        rstd = S.sb("rstd", [P, NT])
        xs = S.sb("xs", [P, 2, D])
        sq_done, ms_done, rstd_done, scaled, tr_done, evac_done = (S.sem(n) for n in (
            "sq_done", "ms_done", "rstd_done", "scaled", "tr_done", "evac_done"))
        with nc.Block() as block:
            @block.scalar
            def _(act):
                for t in tiles:
                    n = rows_of(t)
                    if wait_x is not None:
                        act.wait_ge(*wait_x(t))
                    if t:
                        act.wait_ge(sq_done, t)
                    nc.scalar.activation(junk[0:n, :], X[0:n, t, :], ACT.Square,
                                         accum_out=ss[0:n, t:t + 1]).then_inc(sq_done, 1)

            @block.gpsimd
            def _(pool):
                for t in tiles:
                    n = rows_of(t)
                    pool.wait_ge(sq_done, t + 1)
                    nc.gpsimd.tensor_scalar(ms[0:n, t:t + 1], ss[0:n, t:t + 1], 1.0 / D, EPS,
                                            ALU.mult, ALU.add).then_inc(ms_done, 1)
                    pool.wait_ge(ms_done, t + 1)
                    nc.gpsimd.tensor_tensor(rstd[0:n, t:t + 1], ms[0:n, t:t + 1], M.neg_half[0:n, 0:1],
                                            ALU.pow).then_inc(rstd_done, 1)

            @block.vector
            def _(dve):
                def evacuate(t):
                    n = rows_of(t)
                    dve.wait_ge(tr_done, t + 1)
                    for b in range(2):
                        last = nc.vector.tensor_tensor(
                            out[:, 4 * b:4 * b + 4, t * P:t * P + n],
                            M.PS[:, 2 * (t % 2) + b, 0:4 * n].rearrange("p (c n) -> p c n", c=4),
                            M.cols[:, col + 4 * b:col + 4 * b + 4].unsqueeze(2).to_broadcast([P, 4, n]), ALU.mult)
                    last.then_inc(evac_done, 1)
                for t in tiles:
                    n = rows_of(t)
                    dve.wait_ge(rstd_done, t + 1)
                    if t >= 2:
                        dve.wait_ge(tr_done, t - 1)
                    nc.vector.tensor_scalar(xs[0:n, t % 2, :], X[0:n, t, :], rstd[0:n, t:t + 1], None,
                                            ALU.mult).then_inc(scaled, 1)
                    if t >= 1:
                        evacuate(t - 1)
                evacuate(tiles[-1])

            @block.tensor
            def _(pe):
                for t in tiles:
                    n = rows_of(t)
                    pe.wait_ge(scaled, t + 1)
                    if t >= 2:
                        pe.wait_ge(evac_done, t - 1)
                    for c in range(KC):
                        last = nc.tensor.transpose(M.PS[:, 2 * (t % 2) + c // 4, (c % 4) * n:(c % 4 + 1) * n],
                                                   xs[0:n, t % 2, c * P:(c + 1) * P], K("ident")[0:n, 0:n])
                    last.then_inc(tr_done, 1)


def projection_stage(nc, M, K, name, XT, kc, tiles, w_dram, chunks, w=None, sq=None):
    steps = [(j, t) for j in range(len(chunks)) for t in tiles]
    T = len(tiles)

    def count(s, f):
        return sum(1 for j, t in steps[:s] if f(chunks[j]))
    normed = lambda s: count(s, lambda c: c.norm is not None)
    turned = lambda s: count(s, lambda c: c.sources is not None)

    def stored(s):
        return sum(16 * len(chunks[j].stores(t, rows_of(t), 0)) for q, (j, t) in enumerate(steps[:s + 1])
                   if q % 2 == s % 2)

    with ExitStack() as ctx:
        S = Stage(nc, ctx, name)
        wmax = max(c.width for c in chunks)
        if w is None:
            w = S.sb("w", [P, 2, kc, wmax])
        nat = S.sb("nat", [P, 2, wmax])
        kd = S.sb("kd", [P, 2, wmax])
        M.nat, M.kd = nat, kd
        if sq is None:
            sq = S.sb("sq", [P, 2, wmax])
        ss = S.sb("ss", [P, 2, 8])
        ms = S.sb("ms", [P, 2, 8])
        rstd = S.sb("rstd", [P, 2, 8])
        w_loaded = [S.sem(f"w_loaded{i}") for i in range(2)]
        store_done = [S.store_sem(f"store_done{i}") for i in range(2)]
        mm_done, act_done, ss_done, ms_done, rstd_done, nat_done, nat_mul, tr_done, evac_done = (
            S.sem(n) for n in ("mm_done", "act_done", "ss_done", "ms_done", "rstd_done", "nat_done",
                               "nat_mul", "tr_done", "evac_done"))

        def wait_nat(eng, s):
            c = chunks[steps[s][0]]
            if c.norm:
                eng.wait_ge(nat_mul, normed(s + 1))
            if c.gains:
                eng.wait_ge(nat_done, count(s + 1, lambda c: c.gains is not None))

        with nc.Block() as block:
            @block.sync
            def _(sp):
                def load(j):
                    if j >= 2:
                        sp.wait_ge(mm_done, (j - 1) * T)
                    c = chunks[j]
                    sp.dma_start(w[:, j % 2, :, 0:c.width],
                                 w_dram[:, c.off:c.off + c.width].rearrange("(k p) n -> p k n", p=P)
                                 ).then_inc(w_loaded[j % 2], 16)
                load(0)
                for s, (j, t) in enumerate(steps):
                    if t == tiles[0] and j + 1 < len(chunks):
                        load(j + 1)
                    pairs = chunks[j].stores(t, rows_of(t), s % 2)
                    if pairs:
                        sp.wait_ge(act_done, s + 1)
                        wait_nat(sp, s)
                    for dst, src in pairs:
                        sp.dma_start(dst, src).then_inc(store_done[s % 2], 16)
                for s in range(max(len(steps) - 2, 0), len(steps)):
                    if stored(s):
                        sp.wait_ge(store_done[s % 2], stored(s))

            @block.tensor
            def _(pe):
                def transposes(s):
                    j, t = steps[s]
                    c = chunks[j]
                    if c.sources is None:
                        return
                    n = rows_of(t)
                    pe.wait_ge(act_done, s + 1)
                    wait_nat(pe, s)
                    k = turned(s)
                    if k >= 2:
                        pe.wait_ge(evac_done, k - 1)
                    for m, src in enumerate(c.sources(t, n, s % 2)):
                        last = nc.tensor.transpose(M.PS[:, 4 + k % 2, m * n:(m + 1) * n], src,
                                                   K("ident")[0:n, 0:n])
                    last.then_inc(tr_done, 1)
                for s, (j, t) in enumerate(steps):
                    n = rows_of(t)
                    if t == tiles[0]:
                        pe.wait_ge(w_loaded[j % 2], 16 * (j // 2 + 1))
                    if s >= 3:
                        pe.wait_ge(act_done, s - 2)
                        if normed(s - 2):
                            pe.wait_ge(nat_mul, normed(s - 2))
                    for c in range(kc):
                        last = nc.tensor.matmul(M.PS[0:n, s % 3, 0:chunks[j].width],
                                                XT[:, c, t * P:t * P + n], w[:, j % 2, c, 0:chunks[j].width],
                                                start=(c == 0), stop=(c == kc - 1))
                    last.then_inc(mm_done, 1)
                    if s >= 1:
                        transposes(s - 1)
                transposes(len(steps) - 1)

            @block.scalar
            def _(act):
                def evacuate(s):
                    j, t = steps[s]
                    c = chunks[j]
                    if c.sources is None:
                        return
                    k = turned(s)
                    act.wait_ge(tr_done, k + 1)
                    for dst, src, gain in c.targets(t, rows_of(t), M.PS[:, 4 + k % 2, :]):
                        if gain is None:
                            last = nc.scalar.copy(dst, src)
                        else:
                            last = nc.scalar.activation(dst, src, ACT.Copy, scale=gain)
                    last.then_inc(evac_done, 1)
                for s, (j, t) in enumerate(steps):
                    c, n = chunks[j], rows_of(t)
                    act.wait_ge(mm_done, s + 1)
                    ps = M.PS[0:n, s % 3, :]
                    last = None
                    if c.norm:
                        if s >= 2 and normed(s - 1):
                            act.wait_ge(ss_done, normed(s - 1))
                        last = nc.scalar.activation(sq[0:n, s % 2, 0:c.norm[0]], ps[:, 0:c.norm[0]], ACT.Square)
                    if c.copies is not None:
                        if s >= 2 and turned(s - 1):
                            act.wait_ge(tr_done, turned(s - 1))
                        if s >= 2 and stored(s - 2):
                            act.wait_ge(store_done[s % 2], stored(s - 2))
                        for dst, src in c.copies(t, n, ps, s % 2):
                            last = nc.scalar.copy(dst, src)
                    last.then_inc(act_done, 1)
                    if s >= 1:
                        evacuate(s - 1)
                evacuate(len(steps) - 1)

            @block.gpsimd
            def _(pool):
                k = 0
                for s, (j, t) in enumerate(steps):
                    c, n = chunks[j], rows_of(t)
                    if not c.norm:
                        continue
                    k += 1
                    h = c.norm[0] // c.norm[1]
                    pool.wait_ge(ss_done, k)
                    nc.gpsimd.tensor_scalar(ms[0:n, s % 2, 0:h], ss[0:n, s % 2, 0:h], 1.0 / c.norm[1], EPS,
                                            ALU.mult, ALU.add).then_inc(ms_done, 1)
                    pool.wait_ge(ms_done, k)
                    nc.gpsimd.tensor_tensor(rstd[0:n, s % 2, 0:h], ms[0:n, s % 2, 0:h], M.neg_half[0:n, 0:h],
                                            ALU.pow).then_inc(rstd_done, 1)

            @block.vector
            def _(dve):
                k = 0
                for s, (j, t) in enumerate(steps):
                    c, n = chunks[j], rows_of(t)
                    if not c.norm:
                        continue
                    k += 1
                    cols, hd = c.norm
                    h = cols // hd
                    dve.wait_ge(act_done, s + 1)
                    nc.vector.tensor_reduce(ss[0:n, s % 2, 0:h],
                                            sq[0:n, s % 2, 0:cols].rearrange("p (h d) -> p h d", d=hd),
                                            axis=AX.X, op=ALU.add).then_inc(ss_done, 1)
                    dve.wait_ge(rstd_done, k)
                    if s >= 2 and turned(s - 1):
                        dve.wait_ge(tr_done, turned(s - 1))
                    if s >= 2 and stored(s - 2):
                        dve.wait_ge(store_done[s % 2], stored(s - 2))
                    o = nat[0:n, s % 2, 0:cols]
                    oo = c.arrange(t, o) if c.arrange else o.rearrange("p (h d) -> p h d", d=hd)
                    i0 = M.PS[0:n, s % 3, 0:cols]
                    i1 = rstd[0:n, s % 2, 0:h]
                    if c.arrange and t == NB:
                        for g in range(2):
                            last = nc.vector.tensor_tensor(
                                oo[:, :, g, :], i0.rearrange("p (g r d) -> p g r d", g=2, d=hd)[:, g],
                                i1[:, 4 * g:4 * g + 4].unsqueeze(2).to_broadcast([n, 4, hd]), ALU.mult)
                    else:
                        last = nc.vector.tensor_tensor(oo, i0.rearrange("p (h d) -> p h d", d=hd),
                                                       i1.unsqueeze(2).to_broadcast([n, h, hd]), ALU.mult)
                    last.then_inc(nat_mul, 1)
                    if c.gains is not None:
                        dve.wait_ge(nat_mul, k)
                        for dst, a, b in c.gains(t, n, s % 2):
                            last = nc.vector.tensor_tensor(dst, a, b, ALU.mult)
                        last.then_inc(nat_done, 1)


def input_chunks(M, io):
    def tok(dram_p, dram_s, t):
        return dram_p[t * P:(t + 1) * P] if t < NB else dram_s
    pa_k = io["p_a_k"][0, 0].rearrange("s g d -> s (g d)")
    pa_v = io["p_a_v"][0, 0].rearrange("s g d -> s (g d)")
    pb_k = io["p_b_k"][0, 0].rearrange("s h c d -> s (h c d)")
    pb_v = io["p_b_v"][0, 0].rearrange("s h d -> s (h d)")
    sa_k = io["s_a_k"][0].rearrange("b t g d -> (b t) (g d)")
    sa_v = io["s_a_v"][0].rearrange("b t g d -> (b t) (g d)")
    sb_k = io["s_b_k"][0].rearrange("b t h c d -> (b t) (h c d)")
    sb_v = io["s_b_v"][0].rearrange("b t h d -> (b t) (h d)")
    si_k = io["s_idx_k"][0].rearrange("b t d -> (b t) d")
    col = lambda n: M.cols[:, COL[n]:COL[n] + 1]

    def qa_targets(t, n, ps):
        if t < NB:
            return [(M.QTA[:, :, t * P:(t + 1) * P], ps.rearrange("p (m n) -> p m n", m=4), col("a_q"))]
        out = []
        for g in range(2):
            s = slice(64 * g, 64 * g + 64)
            for r in range(4):
                h = 4 * g + r
                out.append((M.QBA[s, :, 4 * h:4 * h + 4],
                            ps[s, r * NS:(r + 1) * NS].rearrange("p (b t) -> p b t", t=4), col("a_q")[s]))
        return out

    def four(t, n, s):
        return [M.nat[0:n, s, m * P:(m + 1) * P] for m in range(4)]

    def kav_copies(t, n, ps, s):
        va = M.VA[0:n, t, :] if t < NB else M.VAs[:]
        out = [(va, ps[:, 128:256])]
        q = ps[:, 256:512]
        if t < NB:
            out.append((M.nat[0:n, s, 256:512], q))
        else:
            for e in range(2):
                out.append((M.kdi[:].rearrange("p (h e d) -> p h e d", h=4, e=2)[:, :, e, :],
                            q.rearrange("p (h d) -> p h d", d=HD)))
        return out

    def kav_gains(t, n, s):
        src = M.nat[0:n, s, 0:128].rearrange("p (g d) -> p g d", g=2)
        gain = M.gain_ak[0:n].unsqueeze(1).to_broadcast([n, 2, HD])
        if t < NB:
            dst = M.kd[0:n, s, 0:256].rearrange("p (g e d) -> p g e d", g=2, e=2)
            return [(dst[:, :, e, :], src, gain) for e in range(2)]
        return [(M.kd[0:n, s, 0:128].rearrange("p (g d) -> p g d", g=2), src, gain)]

    def kav_sources(t, n, s):
        if t < NB:
            return [M.kd[0:n, s, 0:128], M.kd[0:n, s, 128:256], M.nat[0:n, s, 256:384], M.nat[0:n, s, 384:512]]
        return [M.kd[0:n, s, 0:128]] + [M.kdi[:, h * P:(h + 1) * P] for h in range(4)]

    def kav_targets(t, n, ps):
        if t < NB:
            sl = slice(t * P, (t + 1) * P)
            return [(M.KTA[:, :, sl], ps[:, 0:256].rearrange("p (m n) -> p m n", m=2), None),
                    (M.QTI[:, :, sl], ps[:, 256:512].rearrange("p (m n) -> p m n", m=2), None)]
        return [(M.KTAs[:], ps[:, 0:NS], None)] + [
            (M.QBI[:, :, 4 * h:4 * h + 4], ps[:, (1 + h) * NS:(2 + h) * NS].rearrange("p (b t) -> p b t", t=4), None)
            for h in range(4)]

    def kav_stores(t, n, s):
        if t < NB:
            k = M.kd[0:n, s, 0:256].rearrange("p (g e d) -> p g e d", g=2, e=2)[:, :, 0, :]
            return [(pa_k[t * P:(t + 1) * P].rearrange("s (g d) -> s g d", g=2), k),
                    (pa_v[t * P:(t + 1) * P], M.VA[0:n, t, :])]
        return [(sa_k, M.kd[0:n, s, 0:128]), (sa_v, M.VAs[:])]

    def ki_copies(t, n, ps, s):
        wi = M.WI[0:n, t, :] if t < NB else M.WIs[:]
        return [(M.nat[0:n, s, 0:64], ps[:, 0:64]), (M.nat[0:n, s, 64:128], ps[:, 0:64]), (wi, ps[:, 64:68])]

    def ki_targets(t, n, ps):
        return [(M.KTI[:, t * P:(t + 1) * P] if t < NB else M.KTIs[:], ps[:, 0:n], None)]

    def qb_targets(t, n, ps):
        if t < NB:
            return [(M.QTB[:, :, t * P:(t + 1) * P], ps.rearrange("p (m n) -> p m n", m=4), col("b_q"))]
        out = []
        for h in range(4):
            for c in range(2):
                s = slice(64 * c, 64 * c + 64)
                r = 8 * h + 4 * c
                out.append((M.QBB[s, h, :, r:r + 4],
                            ps[s, h * NS:(h + 1) * NS].rearrange("p (b t) -> p b t", t=4), col("b_q")[s]))
        return out

    def kb_gains(t, n, s):
        return [(M.kd[0:n, s, :].rearrange("p (h d) -> p h d", d=HD), M.nat[0:n, s, :].rearrange("p (h d) -> p h d", d=HD),
                 M.gain_bk[0:n].unsqueeze(1).to_broadcast([n, 8, HD]))]

    def kb_targets(t, n, ps):
        if t < NB:
            return [(M.KTB[:, :, t * P:(t + 1) * P], ps.rearrange("p (m n) -> p m n", m=4), None)]
        return [(M.KTBs[:], ps[:, 0:4 * NS].rearrange("p (m n) -> p m n", m=4), None)]

    def vb(t):
        return M.VB[:, t, :] if t < NB else M.VBs[:]

    return [
        Chunk(0, 512, norm=(512, HD), sources=four, targets=qa_targets,
              arrange=lambda t, o: (o.rearrange("p (r g d) -> p r g d", g=2, d=HD) if t == NB
                                    else o.rearrange("p (h d) -> p h d", d=HD))),
        Chunk(512, 512, norm=(128, HD), copies=kav_copies, gains=kav_gains, sources=kav_sources,
              targets=kav_targets, stores=kav_stores),
        Chunk(1024, 68, copies=ki_copies, sources=lambda t, n, s: [M.nat[0:n, s, 0:128]], targets=ki_targets,
              stores=lambda t, n, s: [(tok(io["p_idx_k"][0, 0], si_k, t), M.nat[0:n, s, 0:64])]),
        Chunk(1092, 512, norm=(512, HD), sources=four, targets=qb_targets),
        Chunk(1604, 512, norm=(512, HD), gains=kb_gains,
              sources=lambda t, n, s: [M.kd[0:n, s, m * P:(m + 1) * P] for m in range(4)], targets=kb_targets,
              stores=lambda t, n, s: [(tok(pb_k, sb_k, t), M.kd[0:n, s, :])]),
        Chunk(2116, 512, copies=lambda t, n, ps, s: [(vb(t), ps)],
              stores=lambda t, n, s: [(tok(pb_v, sb_v, t), vb(t))]),
    ]


def prompt_attention_stage(nc, M, K):
    items = [("I", 0, 0)]
    for i in range(NB):
        if i + 1 < NB:
            items.append(("I", i + 1, 0))
        items += [("A", i, h) for h in range(A_H)] + [("B", i, h) for h in range(B_H)]
        items.append(("M", i, 0))
    order = []
    late = []
    for it in items:
        if it[0] == "M":
            late.append([it, 3])
            continue
        order.append(it)
        for l in late:
            l[1] -= 1
        while late and late[0][1] <= 0:
            order.append(late.pop(0)[0])
    order += [l[0] for l in late]
    items = order
    units_of = {"I": IDX_H, "A": 1, "B": 2, "M": 0}
    unit0, u = [], 0
    for kind, i, h in items:
        unit0.append(u)
        u += units_of[kind]

    def groups(kind, i):
        n = {"I": 0, "M": KC}.get(kind, i + 1)
        return [list(range(a, min(a + 4, n))) for a in range(0, n, 4)]
    group0, gcount = [], 0
    for kind, i, h in items:
        group0.append(gcount)
        gcount += len(groups(kind, i))
    nth = {}
    for kind in ("I", "A", "B", "M"):
        c = 0
        for n, it in enumerate(items):
            nth[kind, n] = c
            c += it[0] == kind
    head_no = lambda n: nth["A", n] + nth["B", n]
    exps = lambda n: nth["A", n] + 2 * nth["B", n]
    SLICE = 3

    with ExitStack() as ctx:
        S = Stage(nc, ctx, "pa")
        relu = M.X[:, 6:8, :]
        score = S.sb("score", [P, 2, SEQ])
        work = S.sb("work", [P, SEQ])
        top8 = S.sb("top8", [P, 8])
        mask = S.sb("mask", [P, 2, SEQ], BF16)
        prob = M.X[:, 0:4, :]
        comb = M.X[:, 4:6, :]
        pt = S.sb("pt", [P, 2, NB, P])
        negmax = S.sb("negmax", [P, 4])
        psum_ = S.sb("psum", [P, 4])
        rsum = S.sb("rsum", [P, 8])
        osq = S.sb("osq", [P, P])
        oss = S.sb("oss", [P, 2])
        oms = S.sb("oms", [P, 2])
        ors = S.sb("ors", [P, 2])
        mix = S.sb("mix", [P, 2, D])
        (s_ready, s_used, relu_used, max_done, mask_done, comb_done, tr_done, pt_ready, pv_done, o_sq,
         o_ms, o_rstd, o_done, chain, rs_done) = (S.sem(n) for n in (
             "s_ready", "s_used", "relu_used", "max_done", "mask_done", "comb_done", "tr_done", "pt_ready",
             "pv_done", "o_sq", "o_ms", "o_rstd", "o_done", "chain", "rs_done"))

        def slot(u, a, b):
            return M.PS[:, 2 * (u % 2):2 * (u % 2) + 2, :].rearrange("p b n -> p (b n)")[:, a:b]

        def parts(a, b):
            return [(x, min(b, (x // CH + 1) * CH)) for x in [a] + [y for y in range(CH, b, CH) if y > a]]

        with nc.Block() as block:
            @block.tensor
            def _(pe):
                def logits(n):
                    kind, i, h = items[n]
                    nk = (i + 1) * P
                    qs = slice(i * P, (i + 1) * P)
                    for k in range(units_of[kind]):
                        u = unit0[n] + k
                        if u >= 2:
                            pe.wait_ge(s_used, u - 1)
                        if kind == "A":
                            if k == 0 and h == 0:
                                pe.wait_ge(mask_done, i + 1)
                            s = slice(64 * (h % 2), 64 * (h % 2) + 64)
                            q, key = M.QTA[s, h // 2, qs], M.KTA[s, h // 4, :]
                        elif kind == "B":
                            s = slice(64 * k, 64 * k + 64)
                            q, key = M.QTB[s, h, qs], M.KTB[s, h, :]
                        else:
                            s = slice(64 * (k % 2), 64 * (k % 2) + 64)
                            q, key = M.QTI[s, k // 2, qs], M.KTI[s, :]
                        for a, b in parts(0, nk):
                            last = nc.tensor.matmul(slot(u, a, b), q, key[:, a:b], start=True, stop=True)
                        if kind == "A":
                            for a, b in parts(0, nk):
                                last = nc.tensor.matmul(slot(u, a, b), M.ident_b[:], mask[:, i % 2, a:b],
                                                        start=False, stop=True, skip_group_check=True)
                        if kind != "I":
                            hb = h if kind == "A" else A_H + h
                            lo = max(0, nk - 2 * P)
                            for a, b in parts(lo, nk):
                                o = 2 * P - nk
                                last = nc.tensor.matmul(slot(u, a, b), K("ident"), M.bias_p[:, hb, a + o:b + o],
                                                        start=False, stop=True, skip_group_check=True)
                        last.then_inc(s_ready, 1)

                def transposes(n):
                    kind, i, h = items[n]
                    if kind == "I":
                        return
                    if kind == "A":
                        pe.wait_ge(s_used, unit0[n] + 1)
                        src = prob[:, exps(n) % 4, :]
                    elif kind == "B":
                        pe.wait_ge(comb_done, nth["B", n] + 1)
                        src = comb[:, nth["B", n] % 2, :]
                    else:
                        pe.wait_ge(o_done, 12 * (i + 1))
                        src = mix[:, i % 2, :]
                    for x, blocks in enumerate(groups(kind, i)):
                        gi = group0[n] + x
                        if gi >= 2:
                            pe.wait_ge(pt_ready, gi - 1)
                        for y, kb in enumerate(blocks):
                            last = nc.tensor.transpose(M.PS[:, 4 + gi % 2, y * P:(y + 1) * P],
                                                       src[:, kb * P:(kb + 1) * P], K("ident"))
                        last.then_inc(tr_done, 1)

                def values(n):
                    kind, i, h = items[n]
                    if kind in ("I", "M"):
                        return
                    hn = head_no(n)
                    if hn >= 2:
                        pe.wait_ge(o_done, hn - 1)
                    w = HD if kind == "A" else 2 * HD
                    for x, blocks in enumerate(groups(kind, i)):
                        pe.wait_ge(pt_ready, group0[n] + x + 1)
                        for kb in blocks:
                            v = M.VA[:, kb, (h // 4) * HD:(h // 4 + 1) * HD] if kind == "A" else \
                                M.VB[:, kb, h * P:(h + 1) * P]
                            last = nc.tensor.matmul(M.PS[:, 6 + hn % 2, 0:w], pt[:, hn % 2, kb, :], v,
                                                    start=(kb == 0), stop=(kb == i))
                    last.then_inc(pv_done, 1)

                logits(0)
                for n in range(len(items)):
                    transposes(n)
                    if n + 1 < len(items):
                        logits(n + 1)
                    values(n)

            @block.scalar
            def _(act):
                def out_square(n):
                    if n < 0 or items[n][0] != "B":
                        return
                    b = nth["B", n]
                    act.wait_ge(pv_done, head_no(n) + 1)
                    if b >= 1:
                        act.wait_ge(o_sq, b)
                    nc.scalar.activation(osq[:], M.PS[:, 6 + head_no(n) % 2, 0:P], ACT.Square,
                                         accum_out=oss[:, b % 2:b % 2 + 1]).then_inc(o_sq, 1)
                for n, (kind, i, h) in enumerate(items):
                    nk = (i + 1) * P
                    for k in range(units_of[kind]):
                        u = unit0[n] + k
                        act.wait_ge(s_ready, u + 1)
                        if kind == "I":
                            r = nth["I", n] * IDX_H + k
                            if r >= 2:
                                act.wait_ge(relu_used, r - 1)
                            nc.scalar.activation(relu[:, r % 2, 0:nk], slot(u, 0, nk), ACT.Relu,
                                                 scale=HD ** -0.5 * IDX_H ** -0.5).then_inc(s_used, 1)
                        else:
                            e = exps(n) + k
                            act.wait_ge(max_done, e + 1)
                            if e >= 4:
                                act.wait_ge(rs_done, e - 3)
                                m = min(x for x in range(n) if exps(x + 1) > e - 4)
                                if items[m][0] == "A":
                                    act.wait_ge(tr_done, group0[m + 1])
                                else:
                                    act.wait_ge(comb_done, nth["B", m] + 1)
                            nc.scalar.activation(prob[:, e % 4, 0:nk], slot(u, 0, nk), ACT.Exp,
                                                 bias=negmax[:, e % 4:e % 4 + 1],
                                                 accum_out=psum_[:, e % 4:e % 4 + 1]).then_inc(s_used, 1)
                    out_square(n - 1)
                    for x, blocks in enumerate(groups(kind, i)):
                        gi = group0[n] + x
                        act.wait_ge(tr_done, gi + 1)
                        m = len(blocks)
                        src = M.PS[:, 4 + gi % 2, 0:m * P].rearrange("p (k q) -> p k q", k=m)
                        if kind == "M":
                            dst = (M.QTA if x == 0 else M.QTB)[:, :, i * P:(i + 1) * P]
                        else:
                            hn = head_no(n)
                            if hn >= 2:
                                act.wait_ge(pv_done, hn - 1)
                            dst = pt[:, hn % 2, blocks[0]:blocks[0] + m, :]
                        nc.scalar.copy(dst, src).then_inc(pt_ready, 1)
                out_square(len(items) - 1)

            @block.gpsimd
            def _(pool):
                for b in range(NB * B_H):
                    pool.wait_ge(o_sq, b + 1)
                    nc.gpsimd.tensor_scalar(oms[:, b % 2:b % 2 + 1], oss[:, b % 2:b % 2 + 1], 1.0 / (2 * HD), EPS,
                                            ALU.mult, ALU.add).then_inc(o_ms, 1)
                    pool.wait_ge(o_ms, b + 1)
                    nc.gpsimd.tensor_tensor(ors[:, b % 2:b % 2 + 1], oms[:, b % 2:b % 2 + 1], M.neg_half[:, 0:1],
                                            ALU.pow).then_inc(o_rstd, 1)

            @block.vector
            def _(dve):
                link = Chain(dve, chain)
                topk = {"left": 0, "i": 0}

                def topk_slice(count):
                    i = topk["i"]
                    nk = (i + 1) * P
                    for _ in range(min(count, topk["left"])):
                        link(nc.vector.max(top8[:], work[:, 0:nk]))
                        link(nc.vector.match_replace(work[:, 0:nk], top8[:], work[:, 0:nk], GONE))
                        topk["left"] -= 1
                        if topk["left"] == 0:
                            if i >= 2:
                                dve_wait_mask(i)
                            link(nc.vector.tensor_tensor(work[:, 0:nk], work[:, 0:nk], score[:, i % 2, 0:nk],
                                                         ALU.is_equal))
                            nc.vector.tensor_scalar(mask[:, i % 2, 0:nk], work[:, 0:nk], NEG, None,
                                                    ALU.mult).then_inc(mask_done, 1)

                def dve_wait_mask(i):
                    last = max(n for n, it in enumerate(items) if it[0] == "A" and it[1] == i - 2)
                    dve.wait_ge(s_ready, unit0[last] + 1)

                def output(n):
                    if n < 0 or items[n][0] not in ("A", "B"):
                        return
                    kind, i, h = items[n]
                    hn = head_no(n)
                    if h == 0 and kind == "A" and i >= 2:
                        m = [x for x, it in enumerate(items) if it == ("M", i - 2, 0)][0]
                        dve.wait_ge(tr_done, group0[m] + 2)
                    if kind == "A":
                        dve.wait_ge(pv_done, hn + 1)
                        dve.wait_ge(rs_done, exps(n) + 1)
                        nc.vector.tensor_scalar(mix[:, i % 2, h * HD:(h + 1) * HD], M.PS[:, 6 + hn % 2, 0:HD],
                                                rsum[:, exps(n) % 8:exps(n) % 8 + 1], None,
                                                ALU.mult).then_inc(o_done, 1)
                    else:
                        b = nth["B", n]
                        dve.wait_ge(o_rstd, b + 1)
                        nc.vector.scalar_tensor_tensor(
                            mix[:, i % 2, A_H * HD + h * P:A_H * HD + (h + 1) * P], M.PS[:, 6 + hn % 2, 0:P],
                            ors[:, b % 2:b % 2 + 1], M.gain_sub[:], ALU.mult, ALU.mult).then_inc(o_done, 1)

                pending = []
                for n, (kind, i, h) in enumerate(items):
                    nk = (i + 1) * P
                    if kind == "I":
                        for k in range(IDX_H):
                            dve.wait_ge(s_used, unit0[n] + k + 1)
                            r = nth["I", n] * IDX_H + k
                            sc = score[:, i % 2, 0:nk]
                            if k == 0:
                                ins = nc.vector.tensor_scalar(sc, relu[:, r % 2, 0:nk], M.WI[:, i, 0:1], None,
                                                              ALU.mult)
                            else:
                                ins = nc.vector.scalar_tensor_tensor(sc, relu[:, r % 2, 0:nk], M.WI[:, i, k:k + 1],
                                                                     sc, ALU.mult, ALU.add)
                            ins.then_inc(relu_used, 1)
                            dve.wait_ge(relu_used, r + 1)
                        diag = slice(i * P, nk)
                        link(nc.vector.tensor_tensor(score[:, i % 2, diag], score[:, i % 2, diag], K("causal"),
                                                     ALU.add))
                        if i < 2:
                            if i:
                                link(nc.vector.memset(mask[:, i % 2, 0:i * P], 0.0))
                            nc.vector.tensor_copy(mask[:, i % 2, diag], K("causal")).then_inc(mask_done, 1)
                        else:
                            link(nc.vector.tensor_copy(work[:, 0:nk], score[:, i % 2, 0:nk]))
                            topk["left"], topk["i"] = TOPK // 8, i
                    elif kind in ("A", "B"):
                        for k in range(units_of[kind]):
                            e = exps(n) + k
                            dve.wait_ge(s_ready, unit0[n] + k + 1)
                            nc.vector.tensor_reduce(negmax[:, e % 4:e % 4 + 1], slot(unit0[n] + k, 0, nk), axis=AX.X,
                                                    op=ALU.max, negate=True).then_inc(max_done, 1)
                        if kind == "B":
                            e, b = exps(n), nth["B", n]
                            for k in range(2):
                                dve.wait_ge(s_used, unit0[n] + k + 1)
                                r = rsum[:, (e + k) % 8:(e + k) % 8 + 1]
                                nc.vector.reciprocal(r, psum_[:, (e + k) % 4:(e + k) % 4 + 1]).then_inc(rs_done, 1)
                                dve.wait_ge(rs_done, e + k + 1)
                                if k:
                                    link(nc.vector.tensor_tensor(r, r, M.neg_lam[:], ALU.mult))
                            if b >= 2:
                                m = [x for x in range(n) if items[x][0] == "B"][b - 2]
                                dve.wait_ge(tr_done, group0[m + 1])
                            p0, p1 = prob[:, e % 4, 0:nk], prob[:, (e + 1) % 4, 0:nk]
                            link(nc.vector.tensor_scalar(p1, p1, rsum[:, (e + 1) % 8:(e + 1) % 8 + 1], None, ALU.mult))
                            nc.vector.scalar_tensor_tensor(comb[:, b % 2, 0:nk], p0, rsum[:, e % 8:e % 8 + 1], p1,
                                                           ALU.mult, ALU.add).then_inc(comb_done, 1)
                        else:
                            e = exps(n)
                            dve.wait_ge(s_used, unit0[n] + 1)
                            nc.vector.reciprocal(rsum[:, e % 8:e % 8 + 1], psum_[:, e % 4:e % 4 + 1]).then_inc(rs_done, 1)
                    output(n - 1)
                    if kind in ("A", "B"):
                        last_head = kind == "B" and h == B_H - 1
                        topk_slice(TOPK if last_head else SLICE)
                output(len(items) - 1)


def sample_index_stage(nc, io, M, K):
    units = [(g, c, j) for g in range(2) for c in range(NCH) for j in range(4)]
    pool_rows = io["cache_idx_k"][0].rearrange("n (s r) d -> (n s) (r d)", r=RK)
    with ExitStack() as ctx:
        S = Stage(nc, ctx, "si")
        kt_n = S.sb("keys", [P, 4, RK * HD])
        kt = S.sb("keys_t", [P, 2, 2, P])
        rel = S.sb("relu", [P, 2, KEYS_S])
        whp = S.sb("w_head", [P, 2, 4])
        wrow = S.sb("w_row", [P, 2])
        wsel = S.sb("w_sel", [P, 2, NS])
        loaded = [S.sem(f"loaded{i}") for i in range(4)]
        tr_done, kt_ready, s_done, relu_done, w_mm, w_ready, chain, sc_mm, sc_done = (S.sem(n) for n in (
            "tr_done", "kt_ready", "s_done", "relu_done", "w_mm", "w_ready", "chain", "sc_mm", "sc_done"))
        pieces = [(g, c) for g in range(2) for c in range(NCH + 1)]

        with nc.Block() as block:
            @block.sync
            def _(sp):
                load_x(sp, io, M)

            @block.gpsimd
            def _(pool):
                for u, (g, c, j) in enumerate(units):
                    if u >= 4:
                        pool.wait_ge(tr_done, u - 3)
                    col = (4 * g + j) * NCH + c
                    nc.gpsimd.indirect_dma_start(
                        kt_n[:, u % 4, :], None, pool_rows,
                        bass.IndirectOffsetOnAxis(ap=M.gather_row[:, col:col + 1], axis=0)).then_inc(loaded[u % 4], 16)

            @block.tensor
            def _(pe):
                for g in range(2):
                    last = nc.tensor.matmul(M.PS[:, 2, 4 * g:4 * g + 4], K(f"tok_to_row{g}"), M.WIs[:],
                                            start=True, stop=True)
                last.then_inc(w_mm, 1)

                def logits(u):
                    g, c, j = units[u]
                    n = g * (NCH + 1) + c
                    pe.wait_ge(kt_ready, u + 1)
                    if j == 0 and n >= 2:
                        pe.wait_ge(relu_done, n - 1)
                    for e in range(2):
                        s = slice(64 * e, 64 * e + 64)
                        last = nc.tensor.matmul(
                            M.PS[32 * j:32 * j + 32, 4 + 2 * (n % 2) + e, 0:256],
                            M.QBI[s, 4 * g + j, :], kt[s, u % 2].rearrange("p a b -> p (a b)"),
                            start=True, stop=True)
                    last.then_inc(s_done, 1)
                    if c == NCH - 1 and j == 3:
                        n += 1
                        if n >= 2:
                            pe.wait_ge(relu_done, n - 1)
                        nc.tensor.matmul(M.PS[:, 4 + 2 * (n % 2), 0:NS],
                                         M.QBI[0:64, 4 * g:4 * g + 4, :].rearrange("p b r -> p (b r)"),
                                         M.KTIs[0:64, :], start=True, stop=True).then_inc(s_done, 1)
                for u in range(len(units)):
                    pe.wait_ge(loaded[u % 4], 16 * (u // 4 + 1))
                    if u >= 2:
                        pe.wait_ge(kt_ready, u - 1)
                    for a in range(2):
                        last = nc.tensor.transpose(M.PS[:, u % 2, a * P:(a + 1) * P],
                                                   kt_n[:, u % 4, a * P:(a + 1) * P], K("ident"))
                    last.then_inc(tr_done, 1)
                    if u >= 1:
                        logits(u - 1)
                logits(len(units) - 1)
                pe.wait_ge(relu_done, len(pieces))
                pe.wait_ge(w_ready, 1)
                for c in range(NCH + 1):
                    w = CH if c < NCH else NS
                    if c >= 2:
                        pe.wait_ge(sc_done, c - 1)
                    for g in range(2):
                        last = nc.tensor.matmul(M.PS[0:NS, 2 + c % 2, 0:w], wsel[:, g, :],
                                                rel[:, g, c * CH:c * CH + w], start=(g == 0), stop=(g == 1))
                    last.then_inc(sc_mm, 1)

            @block.scalar
            def _(act):
                def relu(n):
                    g, c = pieces[n]
                    act.wait_ge(s_done, 33 * g + (4 * (c + 1) if c < NCH else 33))
                    if c < NCH:
                        dst = rel[:, g, c * CH:(c + 1) * CH].rearrange("p (q a e) -> p e a q", a=2, e=2)
                        src = M.PS[:, 4 + 2 * (n % 2):6 + 2 * (n % 2), 0:256].rearrange("p e (a q) -> p e a q", a=2)
                    else:
                        dst, src = rel[:, g, PAST:KEYS_S], M.PS[:, 4 + 2 * (n % 2), 0:NS]
                    nc.scalar.activation(dst, src, ACT.Relu, scale=HD ** -0.5 * IDX_H ** -0.5).then_inc(relu_done, 1)
                for u, (g, c, j) in enumerate(units):
                    act.wait_ge(tr_done, u + 1)
                    if u >= 2:
                        act.wait_ge(s_done, u - 1 + (u - 1 > 32))
                    nc.scalar.copy(kt[:, u % 2].rearrange("p a b -> p (a b)"), M.PS[:, u % 2, 0:2 * P]).then_inc(kt_ready, 1)
                    n = g * (NCH + 1) + c
                    if j == 0 and n >= 1:
                        if c == 0:
                            relu(n - 2)
                        relu(n - 1)
                relu(len(pieces) - 2)
                relu(len(pieces) - 1)
                for c in range(NCH + 1):
                    w = CH if c < NCH else NS
                    act.wait_ge(sc_mm, c + 1)
                    nc.scalar.copy(M.score_s[:, c * CH:c * CH + w], M.PS[0:NS, 2 + c % 2, 0:w]).then_inc(sc_done, 1)

            @block.vector
            def _(dve):
                link = Chain(dve, chain)
                dve.wait_ge(w_mm, 1)
                for g in range(2):
                    link(nc.vector.tensor_tensor(whp[:, g, :], M.PS[:, 2, 4 * g:4 * g + 4], K("head_i"), ALU.mult))
                link(nc.vector.tensor_reduce(wrow[:], whp[:], axis=AX.X, op=ALU.add))
                for g in range(2):
                    last = nc.vector.tensor_scalar(wsel[:, g, :], K(f"row_to_tok{g}"), wrow[:, g:g + 1], None, ALU.mult)
                last.then_inc(w_ready, 1)
                dve.wait_ge(sc_done, NCH + 1)
                link(nc.vector.tensor_tensor(M.score_s[:, PAST:KEYS_S], M.score_s[:, PAST:KEYS_S], K("idx_mask"),
                                             ALU.add))
                link(nc.vector.tensor_copy(M.work_s[:], M.score_s[:]))


def sample_attention_stage(nc, io, M, K, kind):
    sparse = kind == "A"
    kw = A_KV * HD if sparse else B_H * 2 * HD
    nm = kw // P
    cache_k, cache_v = (io["cache_a_k"], io["cache_a_v"]) if sparse else (io["cache_b_k"], io["cache_b_v"])
    flat = "n (s r) g d -> (n s) (r g d)" if sparse else "n (s r) h c d -> (n s) (r h c d)"
    k_rows = cache_k[0].rearrange(flat, r=RK)
    v_rows = cache_v[0].rearrange("n (s r) g d -> (n s) (r g d)", r=RK)
    units = [(g, c, j) for g in range(2) for c in range(NCH) for j in range(4)]
    loads = [(w, g, c, j) for g in range(2) for w in range(2) for c in range(NCH) for j in range(4)]
    at = {x: n for n, x in enumerate(loads)}
    RING = 3
    q_rows = (lambda b, m: M.QBA[:, b, :]) if sparse else (lambda b, m: M.QBB[:, m, b, :])
    new_kt = (lambda m: M.KTAs[:]) if sparse else (lambda m: M.KTBs[:, m, :])
    new_v = M.VAs if sparse else M.VBs
    bk = 0 if sparse else 1
    PG = NCH + 1
    with ExitStack() as ctx:
        S = Stage(nc, ctx, f"s{kind}")
        kv = S.sb("kv", [P, RING, RK * kw])
        kt = S.sb("keys_t", [P, 2, nm, CH])
        prob = S.sb("prob", [P, KEYS_S])
        pmax = S.sb("pmax", [P, PG])
        nmax = S.sb("nmax", [P, 1])
        tot = S.sb("tot", [P, 1])
        coef = S.sb("coef", [P, 1])
        pt = S.sb("pt", [P, 2, RK, P])
        ptn = S.sb("ptn", [NS, P])
        om = S.sb("om", [P, 512])
        top8 = S.sb("top8", [NS, 8])
        oss = S.sb("oss", [NS, 4])
        osq = S.sb("osq", [NS, 512])
        oms = S.sb("oms", [NS, 4])
        ors = S.sb("ors", [NS, 4])
        loaded = [S.sem(f"loaded{i}") for i in range(RING)]
        (bank_full, bank_read, s_done, piece_done, copied, nmax_done, p_ready, pv_unit, o_ready,
         om_ready, o_mm, chain, o_ss, o_ms, o_rs) = (S.sem(n) for n in (
             "bank_full", "bank_read", "s_done", "piece_done", "copied", "nmax_done", "p_ready",
             "pv_unit", "o_ready", "om_ready", "o_mm", "chain", "o_ss", "o_ms", "o_rs"))
        tb, tbank = 0, {}
        for g in range(2):
            for c in range(NCH):
                for j in range(4):
                    for m in range(nm):
                        tbank["k", g, c, j, m] = tb
                        tb += 1
            for c in range(PG):
                tbank["p", g, c] = tb
                tb += 1

        def pieces_before(n):
            return sum(sparse + (x % PG >= NCH - 1) for x in range(n + 1))

        with nc.Block() as block:
            @block.gpsimd
            def _(pool):
                for n, (w, g, c, j) in enumerate(loads):
                    if n >= RING:
                        wo, go, co, jo = loads[n - RING]
                        if wo:
                            pool.wait_ge(pv_unit, (go * NCH + co) * 4 + jo + 1)
                        else:
                            pool.wait_ge(bank_full, tbank["k", go, co, jo, nm - 1] + 1)
                    col = (4 * g + j) * NCH + c
                    nc.gpsimd.indirect_dma_start(
                        kv[:, n % RING, :], None, v_rows if w else k_rows,
                        bass.IndirectOffsetOnAxis(ap=M.gather_row[:, col:col + 1], axis=0)
                    ).then_inc(loaded[n % RING], 16)
                if not sparse:
                    pool.wait_ge(o_ss, 1)
                    nc.gpsimd.tensor_scalar(oms[:], oss[:], 1.0 / (2 * HD), EPS, ALU.mult, ALU.add).then_inc(o_ms, 1)
                    pool.wait_ge(o_ms, 1)
                    nc.gpsimd.tensor_tensor(ors[:], oms[:], M.neg_half[0:NS, 0:4], ALU.pow).then_inc(o_rs, 1)

            @block.tensor
            def _(pe):
                def bank_free(x):
                    if x >= 4:
                        pe.wait_ge(bank_read, x - 3)

                def logits(u):
                    g, c, j = units[u]
                    n = g * PG + c
                    pe.wait_ge(bank_read, tbank["k", g, c, j, nm - 1] + 1)
                    if j == 0 and n >= 2:
                        pe.wait_ge(copied, n - 1)
                    out = M.PS[32 * j:32 * j + 32, 4 + n % 2, :]
                    for m in range(nm):
                        last = nc.tensor.matmul(out, q_rows(4 * g + j, m), kt[:, u % 2, m, :], start=(m == 0),
                                                stop=(m == nm - 1))
                    last.then_inc(s_done, 1)
                    if j < 3:
                        return
                    extra(g, c, n)
                    if c == NCH - 1:
                        n += 1
                        if n >= 2:
                            pe.wait_ge(copied, n - 1)
                        for j in range(4):
                            for m in range(nm):
                                last = nc.tensor.matmul(M.PS[32 * j:32 * j + 32, 4 + n % 2, 0:NS],
                                                        q_rows(4 * g + j, m), new_kt(m), start=(m == 0),
                                                        stop=(m == nm - 1))
                        last.then_inc(s_done, 1)
                        extra(g, NCH, n)

                def extra(g, c, n):
                    w = CH if c < NCH else NS
                    bank = M.PS[:, 4 + n % 2, 0:w]
                    todo = []
                    if sparse:
                        todo.append((bank, M.tok_to_row_b[:, g, :], M.mask_s[:, c * CH:c * CH + w]))
                    if c == NCH - 1:
                        todo.append((M.PS[:, 4 + n % 2, CH - P:CH], K("ident"), M.bias_s[:, bk, :]))
                    if c == NCH:
                        todo.append((bank, K("ident"), M.bias_new[:, bk, g, :]))
                    for o, a, b in todo:
                        nc.tensor.matmul(o, a, b, start=False, stop=True, skip_group_check=True).then_inc(piece_done, 1)


                for g in range(2):
                    for c in range(NCH):
                        for j in range(4):
                            u = (g * NCH + c) * 4 + j
                            n = at[0, g, c, j]
                            pe.wait_ge(loaded[n % RING], 16 * (n // RING + 1))
                            for m in range(nm):
                                x = tbank["k", g, c, j, m]
                                bank_free(x)
                                for r in range(RK):
                                    last = nc.tensor.transpose(
                                        M.PS[:, x % 4, r * P:(r + 1) * P],
                                        kv[:, n % RING, r * kw + m * P:r * kw + (m + 1) * P], K("ident"))
                                last.then_inc(bank_full, 1)
                            if c or j:
                                logits(u - 1)
                    logits(u)
                    pe.wait_ge(p_ready, g + 1)

                    def turn(c):
                        x = tbank["p", g, c]
                        bank_free(x)
                        if c < NCH:
                            for r in range(RK):
                                last = nc.tensor.transpose(M.PS[:, x % 4, r * P:(r + 1) * P],
                                                           prob[:, c * CH + r:(c + 1) * CH:RK], K("ident"))
                        else:
                            last = nc.tensor.transpose(M.PS[0:NS, x % 4, 0:P], prob[:, PAST:KEYS_S], K("ident"))
                        last.then_inc(bank_full, 1)
                    turn(0)
                    for c in range(NCH):
                        turn(c + 1)
                        pe.wait_ge(bank_read, tbank["p", g, c] + 1)
                        for j in range(4):
                            n = at[1, g, c, j]
                            pe.wait_ge(loaded[n % RING], 16 * (n // RING + 1))
                            if c == 0 and j == 0 and g == 1:
                                pe.wait_ge(om_ready, 1)
                            for r in range(RK):
                                last = nc.tensor.matmul(
                                    M.PS[32 * j:32 * j + 32, 6, 0:kw], pt[:, c % 2, r, 32 * j:32 * j + 32],
                                    kv[:, n % RING, r * kw:(r + 1) * kw], start=(c == 0 and r == 0), stop=False)
                            last.then_inc(pv_unit, 1)
                    pe.wait_ge(bank_read, tbank["p", g, NCH] + 1)
                    for j in range(4):
                        last = nc.tensor.matmul(M.PS[32 * j:32 * j + 32, 6, 0:kw], ptn[:, 32 * j:32 * j + 32],
                                                new_v[:], start=False, stop=True)
                    last.then_inc(o_ready, 1)
                    pe.wait_ge(om_ready, g + 1)
                    nc.tensor.matmul(M.PS[0:NS, 7, :], K(f"row_to_tok{g}"), om[:], start=(g == 0),
                                     stop=(g == 1)).then_inc(o_mm, 1)

            @block.scalar
            def _(act):
                for g in range(2):
                    for c in range(NCH):
                        for j in range(4):
                            u = (g * NCH + c) * 4 + j
                            if u >= 2:
                                act.wait_ge(s_done, u - 1 + (u - 1 > 32))
                            for m in range(nm):
                                x = tbank["k", g, c, j, m]
                                act.wait_ge(bank_full, x + 1)
                                nc.scalar.copy(kt[:, u % 2, m, :].rearrange("p (q r) -> p r q", r=RK),
                                               M.PS[:, x % 4, :].rearrange("p (r q) -> p r q", r=RK)
                                               ).then_inc(bank_read, 1)
                    act.wait_ge(nmax_done, g + 1)
                    nc.scalar.activation(prob[:], prob[:], ACT.Exp, bias=nmax[:], accum_out=tot[:]).then_inc(p_ready, 1)
                    for c in range(PG):
                        x = tbank["p", g, c]
                        act.wait_ge(bank_full, x + 1)
                        if c >= 2:
                            act.wait_ge(pv_unit, (g * NCH + c - 2) * 4 + 4)
                        if c < NCH:
                            nc.scalar.copy(pt[:, c % 2].rearrange("p r q -> p (r q)"), M.PS[:, x % 4, :]
                                           ).then_inc(bank_read, 1)
                        else:
                            nc.scalar.copy(ptn[:], M.PS[0:NS, x % 4, 0:P]).then_inc(bank_read, 1)

            @block.vector
            def _(dve):
                link = Chain(dve, chain)
                left = [0 if sparse else TOPK // 8]

                def topk_slice(count):
                    for _ in range(min(count, left[0])):
                        link(nc.vector.max(top8[:], M.work_s[:]))
                        link(nc.vector.match_replace(M.work_s[:], top8[:], M.work_s[:], GONE))
                        left[0] -= 1
                for g in range(2):
                    if g == 1:
                        dve.wait_ge(bank_full, tbank["p", 0, NCH] + 1)
                    for c in range(PG):
                        n = g * PG + c
                        w = CH if c < NCH else NS
                        dve.wait_ge(s_done, 33 * g + (4 * (c + 1) if c < NCH else 33))
                        if pieces_before(n):
                            dve.wait_ge(piece_done, pieces_before(n))
                        nc.vector.tensor_scalar(prob[:, c * CH:c * CH + w], M.PS[:, 4 + n % 2, 0:w], 1.0, None,
                                                ALU.mult, ALU.max, accum_out=pmax[:, c:c + 1]).then_inc(copied, 1)
                        topk_slice(2)
                    dve.wait_ge(copied, (g + 1) * PG)
                    nc.vector.tensor_reduce(nmax[:], pmax[:], axis=AX.X, op=ALU.max, negate=True).then_inc(nmax_done, 1)
                    topk_slice(TOPK if g else 0)
                    dve.wait_ge(p_ready, g + 1)
                    link(nc.vector.reciprocal(coef[:], tot[:]))
                    if not sparse:
                        link(nc.vector.tensor_tensor(coef[:], coef[:], M.branch_coef[:], ALU.mult))
                    dve.wait_ge(o_ready, g + 1)
                    if g:
                        dve.wait_ge(o_mm, 1)
                    o = M.PS[:, 6, 0:kw]
                    if sparse:
                        for kvh in range(2):
                            last = nc.vector.scalar_tensor_tensor(
                                om[:, kvh * 256:(kvh + 1) * 256].rearrange("p (h d) -> p h d", d=HD),
                                o[:, kvh * HD:(kvh + 1) * HD].unsqueeze(1).to_broadcast([P, 4, HD]), coef[:],
                                K("head_a")[:, 4 * kvh:4 * kvh + 4].unsqueeze(2).to_broadcast([P, 4, HD]),
                                ALU.mult, ALU.mult)
                    else:
                        last = nc.vector.scalar_tensor_tensor(
                            om[:].rearrange("p (h d) -> p h d", h=4), o.rearrange("p (h d) -> p h d", h=4), coef[:],
                            K("head_b").unsqueeze(2).to_broadcast([P, 4, P]), ALU.mult, ALU.mult)
                    last.then_inc(om_ready, 1)
                dve.wait_ge(o_mm, 2)
                if sparse:
                    link(nc.vector.tensor_copy(M.mix_s[:, 0:512], M.PS[0:NS, 7, :]))
                else:
                    link(nc.vector.tensor_copy(M.mix_s[:, 512:1024], M.PS[0:NS, 7, :]))
                    link(nc.vector.tensor_tensor(osq[:], M.mix_s[:, 512:1024], M.mix_s[:, 512:1024], ALU.mult))
                    nc.vector.tensor_reduce(oss[:], osq[:].rearrange("p (h d) -> p h d", h=4), axis=AX.X,
                                            op=ALU.add).then_inc(o_ss, 1)
                    dve.wait_ge(o_rs, 1)
                    ov = M.mix_s[:, 512:1024].rearrange("p (h d) -> p h d", h=4)
                    link(nc.vector.tensor_tensor(ov, ov, ors[:].unsqueeze(2).to_broadcast([NS, 4, P]), ALU.mult))
                    link(nc.vector.tensor_tensor(ov, ov, M.gain_sub[0:NS].unsqueeze(1).to_broadcast([NS, 4, P]),
                                                 ALU.mult))
                    link(nc.vector.tensor_tensor(M.work_s[:], M.work_s[:], M.score_s[:], ALU.is_equal))
                    link(nc.vector.tensor_scalar(M.mask_s[:], M.work_s[:], NEG, None, ALU.mult))


def sample_mix_stage(nc, M, K, name, src, chunks, out):
    with ExitStack() as ctx:
        S = Stage(nc, ctx, name)
        tr, ev = S.sem("tr"), S.sem("ev")
        with nc.Block() as block:
            @block.tensor
            def _(pe):
                for c in range(chunks):
                    last = nc.tensor.transpose(M.PS[:, 0, c * NS:(c + 1) * NS], src[:, c * P:(c + 1) * P],
                                               K("ident")[0:NS, 0:NS])
                last.then_inc(tr, 1)

            @block.vector
            def _(dve):
                dve.wait_ge(tr, 1)
                for c in range(chunks):
                    last = nc.vector.tensor_copy(out(c), M.PS[:, 0, c * NS:(c + 1) * NS])
                last.then_inc(ev, 1)
                dve.wait_ge(ev, 1)


def residual_stage(nc, M, K, name, lhs, kc, w_dram, ncol, store=None, reloaded=False):
    steps = [(q, t) for q in range(D // ncol) for t in range(NT)]
    with ExitStack() as ctx:
        S = Stage(nc, ctx, name)
        w = S.sb("w", [P, 2, kc, ncol])
        w_loaded = [S.sem(f"w_loaded{i}") for i in range(2)]
        mm_done, added, stored = S.sem("mm_done"), S.sem("added"), S.store_sem("stored")
        with nc.Block() as block:
            @block.sync
            def _(sp):
                def load(q):
                    if q >= 2:
                        sp.wait_ge(mm_done, (q - 1) * NT)
                    sp.dma_start(w[:, q % 2], w_dram[:, q * ncol:(q + 1) * ncol].rearrange("(k p) n -> p k n", p=P)
                                 ).then_inc(w_loaded[q % 2], 16)
                load(0)
                n = 0
                for s, (q, t) in enumerate(steps):
                    if t == 0 and q + 1 < D // ncol:
                        load(q + 1)
                    if store is not None:
                        sp.wait_ge(added, s + 1)
                        sp.dma_start(*store(t, q * ncol, (q + 1) * ncol)).then_inc(stored, 16)
                        n += 16
                if n:
                    sp.wait_ge(stored, n)

            @block.tensor
            def _(pe):
                for s, (q, t) in enumerate(steps):
                    n = rows_of(t)
                    if t == 0:
                        pe.wait_ge(w_loaded[q % 2], 16 * (q // 2 + 1))
                    if s >= 4:
                        pe.wait_ge(added, s - 3)
                    for c in range(kc):
                        last = nc.tensor.matmul(M.PS[0:n, s % 4, 0:ncol], lhs(c, t), w[:, q % 2, c, :],
                                                start=(c == 0), stop=(c == kc - 1))
                    last.then_inc(mm_done, 1)

            @block.vector
            def _(dve):
                for s, (q, t) in enumerate(steps):
                    n = rows_of(t)
                    dve.wait_ge(mm_done, s + 1)
                    if reloaded and q == 0:
                        dve.wait_ge(M.x_loaded[t], 32)
                    x = M.X[0:n, t, q * ncol:(q + 1) * ncol]
                    nc.vector.tensor_tensor(x, M.PS[0:n, s % 4, 0:ncol], x, ALU.add).then_inc(added, 1)


def memory_chunks_kv(M, io):
    mk = io["p_mem_k"][0, 0].rearrange("m h d -> m (h d)")
    mv = io["p_mem_v"][0, 0].rearrange("m h d -> m (h d)")
    return [
        Chunk(0, 512, norm=(512, MEM_D),
              gains=lambda t, n, s: [(M.kd[0:n, s, :].rearrange("p (h d) -> p h d", d=MEM_D),
                                      M.nat[0:n, s, :].rearrange("p (h d) -> p h d", d=MEM_D),
                                      M.gain_mk[0:n].unsqueeze(1).to_broadcast([n, MEM_H, MEM_D]))],
              sources=lambda t, n, s: [M.kd[0:n, s, m * P:(m + 1) * P] for m in range(4)],
              targets=lambda t, n, ps: [(M.KMT[:, :, t * P:(t + 1) * P], ps.rearrange("p (m n) -> p m n", m=4), None)],
              stores=lambda t, n, s: [(mk[t * P:(t + 1) * P], M.kd[0:n, s, :])]),
        Chunk(512, 512, copies=lambda t, n, ps, s: [(M.VM[:, t, :], ps)],
              stores=lambda t, n, s: [(mv[t * P:(t + 1) * P], M.VM[:, t, :])]),
    ]


def memory_chunks_q(M):
    gain = lambda: M.cols[:, COL["mem_q"]:COL["mem_q"] + 1]

    def targets(t, n, ps):
        if t < NB:
            return [(M.QTA[:, :, t * P:(t + 1) * P], ps.rearrange("p (m n) -> p m n", m=4), gain())]
        return [(M.QBM[:, h, :, 4 * h:4 * h + 4], ps[:, h * NS:(h + 1) * NS].rearrange("p (b t) -> p b t", t=4),
                 gain()) for h in range(4)]
    return [Chunk(0, 512, norm=(512, MEM_D),
                  sources=lambda t, n, s: [M.nat[0:n, s, m * P:(m + 1) * P] for m in range(4)], targets=targets)]


def memory_prompt_stage(nc, M, K):
    items = [(t, h) for t in range(NB) for h in range(MEM_H)]
    scale = MEM_D ** -0.5
    with ExitStack() as ctx:
        S = Stage(nc, ctx, "mp")
        prob = S.sb("prob", [P, 2, MEM])
        nm = S.sb("nm", [P, 4])
        tot = S.sb("tot", [P, 2])
        rec = S.sb("rec", [P, 4])
        pt = S.sb("pt", [P, 2, 2 * P])
        om = S.sb("om", [P, 2, 512])
        (s_done, nm_done, chain, p_ready, rec_done, tr_done, pt_ready, pv_done, o_done, ot_tr, ot_done) = (
            S.sem(n) for n in ("s_done", "nm_done", "chain", "p_ready", "rec_done", "tr_done", "pt_ready", "pv_done",
                               "o_done", "ot_tr", "ot_done"))
        with nc.Block() as block:
            @block.tensor
            def _(pe):
                def logits(n):
                    t, h = items[n]
                    if n >= 2:
                        pe.wait_ge(p_ready, n - 1)
                    nc.tensor.matmul(M.PS[:, n % 2, 0:MEM], M.QTA[:, h, t * P:(t + 1) * P], M.KMT[:, h, :],
                                     start=True, stop=True).then_inc(s_done, 1)

                def outputs(t):
                    pe.wait_ge(o_done, 4 * (t + 1))
                    if t >= 2:
                        pe.wait_ge(ot_done, t - 1)
                    for h in range(MEM_H):
                        last = nc.tensor.transpose(M.PS[:, 6 + t % 2, h * P:(h + 1) * P],
                                                   om[:, t % 2, h * P:(h + 1) * P], K("ident"))
                    last.then_inc(ot_tr, 1)
                logits(0)
                for n, (t, h) in enumerate(items):
                    pe.wait_ge(p_ready, n + 1)
                    if n >= 2:
                        pe.wait_ge(pt_ready, n - 1)
                    for a in range(2):
                        last = nc.tensor.transpose(M.PS[:, 2 + n % 2, a * P:(a + 1) * P],
                                                   prob[:, n % 2, a * P:(a + 1) * P], K("ident"))
                    last.then_inc(tr_done, 1)
                    if n + 1 < len(items):
                        logits(n + 1)
                    pe.wait_ge(pt_ready, n + 1)
                    if n >= 2:
                        pe.wait_ge(o_done, n - 1)
                    for a in range(2):
                        last = nc.tensor.matmul(M.PS[:, 4 + n % 2, 0:P], pt[:, n % 2, a * P:(a + 1) * P],
                                                M.VM[:, a, h * P:(h + 1) * P], start=(a == 0), stop=(a == 1))
                    last.then_inc(pv_done, 1)
                    if h == 1 and t >= 1:
                        outputs(t - 1)
                outputs(NB - 1)

            @block.scalar
            def _(act):
                def turned_outputs(t):
                    act.wait_ge(ot_tr, t + 1)
                    nc.scalar.copy(M.QTB[:, :, t * P:(t + 1) * P],
                                   M.PS[:, 6 + t % 2, :].rearrange("p (h q) -> p h q", h=4)).then_inc(ot_done, 1)
                for n, (t, h) in enumerate(items):
                    act.wait_ge(nm_done, n + 1)
                    if n >= 2:
                        act.wait_ge(rec_done, n - 1)
                        act.wait_ge(tr_done, n - 1)
                    nc.scalar.activation(prob[:, n % 2, :], M.PS[:, n % 2, 0:MEM], ACT.Exp, scale=scale,
                                         bias=nm[:, n % 4:n % 4 + 1], accum_out=tot[:, n % 2:n % 2 + 1]
                                         ).then_inc(p_ready, 1)
                    act.wait_ge(tr_done, n + 1)
                    if n >= 2:
                        act.wait_ge(pv_done, n - 1)
                    nc.scalar.copy(pt[:, n % 2, :], M.PS[:, 2 + n % 2, 0:MEM]).then_inc(pt_ready, 1)
                    if h == 2 and t >= 1:
                        turned_outputs(t - 1)
                turned_outputs(NB - 1)

            @block.vector
            def _(dve):
                link = Chain(dve, chain)

                def output(n):
                    t, h = items[n]
                    dve.wait_ge(pv_done, n + 1)
                    dve.wait_ge(rec_done, n + 1)
                    if h == 0 and t >= 2:
                        dve.wait_ge(ot_tr, t - 1)
                    nc.vector.tensor_scalar(om[:, t % 2, h * P:(h + 1) * P], M.PS[:, 4 + n % 2, 0:P],
                                            rec[:, n % 4:n % 4 + 1], None, ALU.mult).then_inc(o_done, 1)
                for n, (t, h) in enumerate(items):
                    m = nm[:, n % 4:n % 4 + 1]
                    dve.wait_ge(s_done, n + 1)
                    link(nc.vector.tensor_reduce(m, M.PS[:, n % 2, 0:MEM], axis=AX.X, op=ALU.max, negate=True))
                    nc.vector.tensor_scalar(m, m, scale, None, ALU.mult).then_inc(nm_done, 1)
                    dve.wait_ge(p_ready, n + 1)
                    nc.vector.reciprocal(rec[:, n % 4:n % 4 + 1], tot[:, n % 2:n % 2 + 1]).then_inc(rec_done, 1)
                    if n:
                        output(n - 1)
                output(len(items) - 1)


def memory_sample_stage(nc, io, M, K):
    seqs = list(range(DEC_B))
    scale = MEM_D ** -0.5
    with ExitStack() as ctx:
        S = Stage(nc, ctx, "ms")
        kn = S.sb("keys", [P, 2, 2, 512])
        vn = S.sb("values", [P, 4, 2, 512])
        kt = S.sb("keys_t", [P, 2, 4, MEM])
        prob = S.sb("prob", [P, MEM])
        nm, tot, rec = S.sb("nm", [P, 1]), S.sb("tot", [P, 1]), S.sb("rec", [P, 1])
        pt = S.sb("pt", [P, 2 * P])
        om = S.sb("om", [P, 512])
        k_loaded = [S.sem(f"k_loaded{i}") for i in range(2)]
        v_loaded = [S.sem(f"v_loaded{i}") for i in range(2)]
        (tr_done, kt_ready, s_done, nm_done, chain, p_ready, pt_tr, pt_ready, o_ready, om_ready, o_mm) = (
            S.sem(n) for n in ("tr_done", "kt_ready", "s_done", "nm_done", "chain", "p_ready", "pt_tr", "pt_ready",
                               "o_ready", "om_ready", "o_mm"))
        with nc.Block() as block:
            @block.sync
            def _(sp):
                for b in seqs:
                    if b >= 2:
                        sp.wait_ge(tr_done, b - 1)
                    sp.dma_start(kn[:, b % 2], io["cache_mem_k"][0, b].rearrange("(a p) h d -> p a (h d)", p=P)
                                 ).then_inc(k_loaded[b % 2], 16)
                    if b % 4 == 0:
                        g = b // 4
                        if g:
                            sp.wait_ge(o_ready, 1)
                        for j in range(4):
                            sp.dma_start(vn[:, j], io["cache_mem_v"][0, b + j].rearrange("(a p) h d -> p a (h d)", p=P)
                                         ).then_inc(v_loaded[g], 16)

            @block.tensor
            def _(pe):
                for b in seqs:
                    g, j = b // 4, b % 4
                    pe.wait_ge(k_loaded[b % 2], 16 * (b // 2 + 1))
                    if b >= 1:
                        pe.wait_ge(kt_ready, b)
                    for h in range(4):
                        for a in range(2):
                            last = nc.tensor.transpose(M.PS[:, h // 2, (h % 2) * MEM + a * P:(h % 2) * MEM + (a + 1) * P],
                                                       kn[:, b % 2, a, h * P:(h + 1) * P], K("ident"))
                    last.then_inc(tr_done, 1)
                    pe.wait_ge(kt_ready, b + 1)
                    if j == 0 and g:
                        pe.wait_ge(p_ready, g)
                    for h in range(4):
                        last = nc.tensor.matmul(M.PS[32 * j:32 * j + 32, 2, 0:MEM], M.QBM[:, h, b, :], kt[:, b % 2, h, :],
                                                start=(h == 0), stop=(h == 3))
                    last.then_inc(s_done, 1)
                    if j < 3:
                        continue
                    pe.wait_ge(p_ready, g + 1)
                    for a in range(2):
                        last = nc.tensor.transpose(M.PS[:, 3, a * P:(a + 1) * P], prob[:, a * P:(a + 1) * P], K("ident"))
                    last.then_inc(pt_tr, 1)
                    pe.wait_ge(pt_ready, g + 1)
                    pe.wait_ge(v_loaded[g], 64)
                    if g:
                        pe.wait_ge(om_ready, g)
                    for jj in range(4):
                        for a in range(2):
                            last = nc.tensor.matmul(M.PS[32 * jj:32 * jj + 32, 4, :],
                                                    pt[:, a * P + 32 * jj:a * P + 32 * jj + 32], vn[:, jj, a, :],
                                                    start=(a == 0), stop=(a == 1))
                    last.then_inc(o_ready, 1)
                    pe.wait_ge(om_ready, g + 1)
                    nc.tensor.matmul(M.PS[0:NS, 5, :], K(f"row_to_tok{g}"), om[:], start=(g == 0),
                                     stop=(g == 1)).then_inc(o_mm, 1)

            @block.scalar
            def _(act):
                for b in seqs:
                    g = b // 4
                    act.wait_ge(tr_done, b + 1)
                    if b >= 2:
                        act.wait_ge(s_done, b - 1)
                    nc.scalar.copy(kt[:, b % 2].rearrange("p (x y) m -> p x (y m)", x=2),
                                   M.PS[:, 0:2, :]).then_inc(kt_ready, 1)
                    if b % 4 == 3:
                        act.wait_ge(nm_done, g + 1)
                        nc.scalar.activation(prob[:], M.PS[:, 2, 0:MEM], ACT.Exp, scale=scale, bias=nm[:],
                                             accum_out=tot[:]).then_inc(p_ready, 1)
                        act.wait_ge(pt_tr, g + 1)
                        nc.scalar.copy(pt[:], M.PS[:, 3, 0:2 * P]).then_inc(pt_ready, 1)

            @block.vector
            def _(dve):
                link = Chain(dve, chain)
                for g in range(2):
                    dve.wait_ge(s_done, 4 * (g + 1))
                    link(nc.vector.tensor_reduce(nm[:], M.PS[:, 2, 0:MEM], axis=AX.X, op=ALU.max, negate=True))
                    nc.vector.tensor_scalar(nm[:], nm[:], scale, None, ALU.mult).then_inc(nm_done, 1)
                    dve.wait_ge(p_ready, g + 1)
                    link(nc.vector.reciprocal(rec[:], tot[:]))
                    dve.wait_ge(o_ready, g + 1)
                    if g:
                        dve.wait_ge(o_mm, g)
                    nc.vector.scalar_tensor_tensor(
                        om[:].rearrange("p (h d) -> p h d", h=4), M.PS[:, 4, :].rearrange("p (h d) -> p h d", h=4), rec[:],
                        K("head_i").unsqueeze(2).to_broadcast([P, 4, P]), ALU.mult, ALU.mult).then_inc(om_ready, 1)
                dve.wait_ge(o_mm, 2)
                link(nc.vector.tensor_copy(M.mem_s[:], M.PS[0:NS, 5, :]))


def ffn_stage(nc, io, M, K, XT, H):
    W = 2 + SEQ + 6 * DEC_B
    WO = W - 2
    S0 = 2 + SEQ
    with ExitStack() as ctx:
        S = Stage(nc, ctx, "ffn")
        wg = S.sb("wg", [P, 2, KC, P])
        wu = S.sb("wu", [P, 2, KC, P])
        gb = S.sb("gb", [P, 2, W])
        gc = S.sb("gc", [P, 2, WO])
        rows = S.sb("rows", [64, DFF])
        state, tails = rows[0:16], rows[32:50]
        tail = S.sb("tail", [P, 18])
        loaded = [S.sem(f"loaded{i}") for i in range(2)]
        (st_loaded, g_mm, u_mm, st_tr, g_ready, tail_ready, tail_tr, tail_out, chain, conv_done, silu_done, h_done,
         zeroed) = (S.sem(n) for n in (
             "st_loaded", "g_mm", "u_mm", "st_tr", "g_ready", "tail_ready", "tail_tr", "tail_out", "chain",
             "conv_done", "silu_done", "h_done", "zeroed"))
        stored = S.store_sem("stored")
        with nc.Block() as block:
            @block.sync
            def _(sp):
                sp.dma_start(state[:], io["state_ffn_conv"][0].rearrange("b w f -> (b w) f")).then_inc(st_loaded, 16)
                for f in range(FT):
                    if f >= 2:
                        sp.wait_ge(u_mm, f - 1)
                    for dst, src in ((wg, io["w_gate"]), (wu, io["w_up"])):
                        sp.dma_start(dst[:, f % 2], src[0, :, f * P:(f + 1) * P].rearrange("(k p) n -> p k n", p=P)
                                     ).then_inc(loaded[f % 2], 16)
                sp.wait_ge(tail_out, FT)
                sp.dma_start(io["p_conv"][0, 0], tails[0:2, :]).then_inc(stored, 16)
                sp.dma_start(io["s_conv"][0].rearrange("b w f -> (b w) f"), tails[2:18, :]).then_inc(stored, 16)
                sp.wait_ge(stored, 32)

            @block.tensor
            def _(pe):
                pe.wait_ge(st_loaded, 16)

                def tail_turn(f):
                    pe.wait_ge(tail_ready, f + 1)
                    if f >= 1:
                        pe.wait_ge(tail_out, f)
                    nc.tensor.transpose(M.PS[0:18, 7, 0:P], tail[:], K("ident")).then_inc(tail_tr, 1)
                for f in range(FT):
                    if f >= 1:
                        pe.wait_ge(g_ready, f)
                    nc.tensor.transpose(M.PS[:, 6, 0:16], state[:, f * P:(f + 1) * P],
                                        K("ident")[0:16, 0:16]).then_inc(st_tr, 1)
                    pe.wait_ge(loaded[f % 2], 32 * (f // 2 + 1))
                    for w, b0, sem in ((wg, 0, g_mm), (wu, 3, u_mm)):
                        if b0 and f >= 1:
                            pe.wait_ge(h_done, f)
                        for c in range(KC):
                            for x, (a, n) in enumerate(((0, 512), (512, 512), (1024, NS))):
                                last = nc.tensor.matmul(M.PS[:, b0 + x, 0:n], w[:, f % 2, c, :], XT[:, c, a:a + n],
                                                        start=(c == 0), stop=(c == KC - 1))
                        last.then_inc(sem, 1)
                        if b0 == 0 and f >= 1:
                            tail_turn(f - 1)
                tail_turn(FT - 1)

            @block.scalar
            def _(act):
                act.wait_ge(zeroed, 1)
                for f in range(FT):
                    b = gb[:, f % 2, :]
                    act.wait_ge(g_mm, f + 1)
                    if f >= 2:
                        act.wait_ge(conv_done, f - 1)
                    nc.scalar.copy(b[:, 2:S0], M.PS[:, 0:2, :].rearrange("p b n -> p (b n)"))
                    seqs = b[:, S0:W].rearrange("p (b x) -> p b x", x=6)
                    nc.scalar.copy(seqs[:, :, 2:6], M.PS[:, 2, 0:NS].rearrange("p (b t) -> p b t", t=4))
                    nc.scalar.copy(seqs[:, :, 0:2], M.PS[:, 6, 0:16].rearrange("p (b w) -> p b w", w=2)
                                   ).then_inc(g_ready, 1)
                    act.wait_ge(g_ready, f + 1)
                    if f >= 1:
                        act.wait_ge(tail_tr, f)
                    nc.scalar.copy(tail[:, 0:2], b[:, SEQ:S0])
                    nc.scalar.copy(tail[:, 2:18].rearrange("p (b w) -> p b w", w=2), seqs[:, :, 4:6]
                                   ).then_inc(tail_ready, 1)
                    act.wait_ge(conv_done, f + 1)
                    nc.scalar.activation(gc[:, f % 2, :], gc[:, f % 2, :], ACT.Silu).then_inc(silu_done, 1)

            @block.vector
            def _(dve):
                link = Chain(dve, chain)
                link(nc.vector.memset(gb[:, 0, 0:2], 0.0))
                nc.vector.memset(gb[:, 1, 0:2], 0.0).then_inc(zeroed, 1)
                for f in range(FT):
                    b, o = gb[:, f % 2, :], gc[:, f % 2, :]
                    cw = lambda j: M.cols[:, COL["conv_w"] + j * FT + f:COL["conv_w"] + j * FT + f + 1]
                    cb = M.cols[:, COL["conv_b"] + f:COL["conv_b"] + f + 1]
                    dve.wait_ge(g_ready, f + 1)
                    link(nc.vector.tensor_scalar(o, b[:, 0:WO], cw(0), cb, ALU.mult, ALU.add))
                    link(nc.vector.scalar_tensor_tensor(o, b[:, 1:1 + WO], cw(1), o, ALU.mult, ALU.add))
                    nc.vector.scalar_tensor_tensor(o, b[:, 2:2 + WO], cw(2), o, ALU.mult, ALU.add).then_inc(conv_done, 1)
                    if f >= 1:
                        finish(nc, dve, f - 1, H, M, gc, silu_done, u_mm, h_done, tail_tr, tail_out, tails, S0)
                finish(nc, dve, FT - 1, H, M, gc, silu_done, u_mm, h_done, tail_tr, tail_out, tails, S0)


def finish(nc, dve, f, H, M, gc, silu_done, u_mm, h_done, tail_tr, tail_out, tails, S0):
    dve.wait_ge(silu_done, f + 1)
    dve.wait_ge(u_mm, f + 1)
    s = gc[:, f % 2, :]
    nc.vector.tensor_tensor(H[:, f, 0:SEQ], M.PS[:, 3:5, :].rearrange("p b n -> p (b n)"), s[:, 0:SEQ], ALU.mult)
    sq = s[:, S0:S0 + 6 * (DEC_B - 1) + 4]
    for b in range(DEC_B):
        last = nc.vector.tensor_tensor(H[:, f, SEQ + 4 * b:SEQ + 4 * b + 4], M.PS[:, 5, 4 * b:4 * b + 4],
                                       sq[:, 6 * b:6 * b + 4], ALU.mult)
    last.then_inc(h_done, 1)
    dve.wait_ge(tail_tr, f + 1)
    nc.vector.tensor_copy(tails[:, f * P:(f + 1) * P], M.PS[0:18, 7, 0:P]).then_inc(tail_out, 1)


def build(nc, io, const_at):
    with ExitStack() as ctx:
        def sb(c, n, shape, dt=F32):
            return c.enter_context(nc.sbuf_tensor(n, shape, dt))
        M = Memory()
        Stage.ended = []
        Stage.stores = {n: ctx.enter_context(nc.semaphore(n)) for n in (
            "in_store_done0", "in_store_done1", "kv_store_done0", "kv_store_done1", "ffn_stored", "dn_stored")}
        M.PS = ctx.enter_context(nc.psum_tensor("PS", [P, 8, 512], F32))
        M.x_loaded = [ctx.enter_context(nc.semaphore(f"x_loaded{t}")) for t in range(NT)]
        M.mem_loaded = ctx.enter_context(nc.semaphore("mem_loaded"))
        M.X = sb(ctx, "X", [P, NT, D])
        ncst = max(o + w for _, o, w in const_at.values())
        M.ident = sb(ctx, "ident_f", [P, P])
        M.cols = sb(ctx, "cols", [P, NCOL])
        M.neg_half = sb(ctx, "neg_half", [P, 16])
        M.neg_lam = sb(ctx, "neg_lam", [P, 1])
        M.zero_col = sb(ctx, "zero_col", [P, 1])

        def K(name):
            if name == "ident":
                return M.ident[:]
            r, o, w = const_at[name]
            return M.const[0:r, o:o + w]

        with ExitStack() as c1:
            M.const = sb(c1, "const", [P, ncst])
            M.ident_b = sb(c1, "ident_b", [P, P], BF16)
            M.tok_to_row_b = sb(c1, "tok_to_row_b", [NS, 2, P], BF16)
            M.gain_ak = sb(c1, "gain_ak", [P, HD])
            M.gain_bk = sb(c1, "gain_bk", [P, HD])
            M.gain_mk = sb(c1, "gain_mk", [P, MEM_D])
            M.gain_sub = sb(c1, "gain_sub", [P, 2 * HD])
            M.branch_coef = sb(c1, "branch_coef", [P, 1])
            M.QTA = sb(c1, "QTA", [P, 4, NTOK])
            M.QTB = sb(c1, "QTB", [P, 4, NTOK])
            M.mem_s = sb(c1, "mem_s", [NS, 512])
            with ExitStack() as c2:
                M.bias_s = sb(c2, "bias_s", [P, 2, P])
                M.bias_new = sb(c2, "bias_new", [P, 2, 2, NS])
                M.gather_row = sb(c2, "gather_row", [P, DEC_B * NCH], I32)
                M.QBA = sb(c2, "QBA", [P, DEC_B, 32])
                M.QBB = sb(c2, "QBB", [P, 4, DEC_B, 32])
                M.QBI = sb(c2, "QBI", [P, DEC_B, 32])
                M.KTAs = sb(c2, "KTAs", [P, NS])
                M.KTBs = sb(c2, "KTBs", [P, 4, NS])
                M.KTIs = sb(c2, "KTIs", [P, NS])
                M.VAs = sb(c2, "VAs", [NS, 128])
                M.VBs = sb(c2, "VBs", [NS, 512])
                M.WIs = sb(c2, "WIs", [NS, 4])
                M.mix_s = sb(c2, "mix_s", [NS, D])
                M.kdi = sb(c2, "kdi", [NS, 512])
                with ExitStack() as c3:
                    M.bias_p = sb(c3, "bias_p", [P, 12, 2 * P])
                    M.QTI = sb(c3, "QTI", [P, 2, SEQ])
                    M.KTA = sb(c3, "KTA", [P, 2, SEQ])
                    M.KTI = sb(c3, "KTI", [P, SEQ])
                    M.KTB = sb(c3, "KTB", [P, 4, SEQ])
                    M.VA = sb(c3, "VA", [P, NB, 128])
                    M.VB = sb(c3, "VB", [P, NB, 512])
                    M.WI = sb(c3, "WI", [P, NB, 4])
                    setup_stage(nc, io, M, K)
                    if STOP == "setup": return
                    with ExitStack() as c4:
                        XT = sb(c4, "XT", [P, KC, NTOK])
                        norm_transpose_stage(nc, M, K, "n1", M.X, range(NT), XT, COL["norm_mix"], lambda t: (M.x_loaded[t], 16))
                        projection_stage(nc, M, K, "in", XT, KC, range(NT), io["w_in"][0], input_chunks(M, io),
                                         M.X[:, 0:8, :].rearrange("p t (e n) -> p (t e) n", n=512)
                                         .rearrange("p (a k) n -> p a k n", a=2),
                                         M.X[:, NB, :].rearrange("p (a n) -> p a n", a=2))
                    if STOP == "proj": return
                    prompt_attention_stage(nc, M, K)
                    if STOP == "pa": return
                with ExitStack() as c3:
                    M.score_s = sb(c3, "score_s", [NS, KEYS_S])
                    M.work_s = sb(c3, "work_s", [NS, KEYS_S])
                    M.mask_s = sb(c3, "mask_s", [NS, KEYS_S], BF16)
                    sample_index_stage(nc, io, M, K)
                    sample_attention_stage(nc, io, M, K, "B")
                    sample_attention_stage(nc, io, M, K, "A")
                sample_mix_stage(nc, M, K, "sx", M.mix_s, KC,
                                 lambda c: (M.QTA if c < 4 else M.QTB)[:, c % 4, SEQ:NTOK])
            if STOP == "sa": return
            clear_semaphores(nc)
            residual_stage(nc, M, K, "wo", lambda c, t: (M.QTA if c < 4 else M.QTB)[:, c % 4, t * P:t * P + rows_of(t)],
                           KC, io["w_out"][0], 512, reloaded=True)
            with ExitStack() as c2:
                M.KMT = sb(c2, "KMT", [P, 4, MEM])
                M.VM = sb(c2, "VM", [P, 2, 512])
                M.QBM = sb(c2, "QBM", [P, 4, DEC_B, 32])
                with ExitStack() as c3:
                    mem = sb(c3, "mem", [P, 2, D])
                    mt = sb(c3, "memT", [P, KC, MEM])
                    with nc.Block() as block:
                        @block.sync
                        def _(sp):
                            sp.dma_start(mem[:], io["mem_prompt"][0].rearrange("(t p) d -> p t d", p=P)
                                         ).then_inc(M.mem_loaded, 16)

                        @block.vector
                        def _(dve):
                            nc.vector.memset(M.QBM[:], 0.0)
                    norm_transpose_stage(nc, M, K, "nm", mem, range(2), mt, COL["norm_mem_src"], lambda t: (M.mem_loaded, 16))
                    projection_stage(nc, M, K, "kv", mt, KC, range(2), io["w_mem_kv"][0], memory_chunks_kv(M, io))
                with ExitStack() as c3:
                    XT = sb(c3, "XT2", [P, KC, NTOK])
                    norm_transpose_stage(nc, M, K, "n2", M.X, range(NT), XT, COL["norm_mem_x"])
                    projection_stage(nc, M, K, "mq", XT, KC, range(NT), io["w_mem_q"][0], memory_chunks_q(M))
                memory_prompt_stage(nc, M, K)
                memory_sample_stage(nc, io, M, K)
                sample_mix_stage(nc, M, K, "sm", M.mem_s, 4, lambda c: M.QTB[:, c, SEQ:NTOK])
            residual_stage(nc, M, K, "mo", lambda c, t: M.QTB[:, c, t * P:t * P + rows_of(t)], 4, io["w_mem_o"][0], 512)
        H = sb(ctx, "H", [P, FT, NTOK])
        with ExitStack() as c1:
            XT = sb(c1, "XT3", [P, KC, NTOK])
            norm_transpose_stage(nc, M, K, "n3", M.X, range(NT), XT, COL["norm_ffn"])
            ffn_stage(nc, io, M, K, XT, H)

        def store(t, a, b):
            if t < NB:
                return io["y_p"][0, t * P:(t + 1) * P, a:b], M.X[:, t, a:b]
            return io["y_s"].rearrange("b t d -> (b t) d")[:, a:b], M.X[0:NS, NB, a:b]
        residual_stage(nc, M, K, "dn", lambda c, t: H[:, c, t * P:t * P + rows_of(t)], FT, io["w_down"][0], 256, store)


STOP = ""
INPUTS = ["x_prompt", "x_sample", "mem_prompt", "cache_a_k", "cache_a_v", "cache_idx_k", "cache_b_k", "cache_b_v",
          "cache_mem_k", "cache_mem_v", "state_ffn_conv", "page_table", "rel_bias", "norm_mix", "w_in", "a_q_norm",
          "a_k_norm", "b_q_norm", "b_k_norm", "diff_lambda", "diff_subln", "w_out", "norm_mem_x", "norm_mem_src",
          "w_mem_q", "w_mem_kv", "mem_q_norm", "mem_k_norm", "w_mem_o", "norm_ffn", "w_up", "w_gate", "ffn_conv_w",
          "ffn_conv_b", "w_down"]
OUTPUTS = [("y_p", (1, SEQ, D)), ("y_s", (DEC_B, DEC_T, D)),
           ("p_a_k", (1, 1, SEQ, A_KV, HD)), ("p_a_v", (1, 1, SEQ, A_KV, HD)), ("p_idx_k", (1, 1, SEQ, HD)),
           ("p_b_k", (1, 1, SEQ, B_H, 2, HD)), ("p_b_v", (1, 1, SEQ, B_H, 2 * HD)),
           ("p_mem_k", (1, 1, MEM, MEM_H, MEM_D)), ("p_mem_v", (1, 1, MEM, MEM_H, MEM_D)), ("p_conv", (1, 1, 2, DFF)),
           ("s_a_k", (1, DEC_B, DEC_T, A_KV, HD)), ("s_a_v", (1, DEC_B, DEC_T, A_KV, HD)),
           ("s_idx_k", (1, DEC_B, DEC_T, HD)), ("s_b_k", (1, DEC_B, DEC_T, B_H, 2, HD)),
           ("s_b_v", (1, DEC_B, DEC_T, B_H, 2 * HD)), ("s_conv", (1, DEC_B, 2, DFF))]


def kernel(**inputs):
    import concourse.bacc as bacc
    from concourse.bass_utils import run_bass_kernel_spmd

    nc = bacc.Bacc("TRN2", target_bir_lowering=False, num_devices=1)
    consts, const_at = pack_constants()
    arrays = {n: np.ascontiguousarray(inputs[n]) for n in INPUTS}
    arrays["consts"] = consts
    arrays["ident"] = np.eye(P, dtype=np.float32)
    io = {n: nc.dram_tensor(n, a.shape, mybir.dt.from_np(a.dtype), kind="ExternalInput").ap()
          for n, a in arrays.items()}
    io.update({n: nc.dram_tensor(n, s, F32, kind="ExternalOutput").ap() for n, s in OUTPUTS})
    build(nc, io, const_at)
    r = run_bass_kernel_spmd(nc, [arrays], core_ids=[0])
    return tuple(r.results[0][n] for n, _ in OUTPUTS)
```
